# Optimizing a Trainium2 kernel written in Bass

```python
import jax, jax.numpy as jnp
from jax import lax
import numpy as np

D_MODEL = 1024
BATCH = 1
SEQ = 1024
DEPTH = 1
DEC_BATCH = 8
DEC_SEQ = 1
PAST_LEN = 4096
PAGE_SIZE = 128

GLA_HEADS = 4
GLA_DK = 64
GLA_DV = 128
GLA_GATE_RANK = 16
GLA_GATE_TEMP = 16.0
GLA_CHUNK = 64
NSA_HEADS = 8
NSA_KV_HEADS = 2
NSA_GROUP = NSA_HEADS // NSA_KV_HEADS
NSA_HEAD_DIM = 64
CMP_LEN = 32
CMP_STRIDE = 16
CMP_HIDDEN = 128
SEL_BLOCK = 64
SEL_TOPK = 16
WINDOW = 512
NSA_QBLK = 64
D_FF = 4 * D_MODEL
EPS = 1e-6
NEG_SCORE = -1e9
FORCE_SCORE = 1e9

GLA_QK_W = GLA_HEADS * GLA_DK
GLA_V_W = GLA_HEADS * GLA_DV
NSA_Q_W = NSA_HEADS * NSA_HEAD_DIM
NSA_KV_W = NSA_KV_HEADS * NSA_HEAD_DIM
MIX_WIDTH = GLA_V_W + NSA_Q_W
IN_SIZES = (GLA_QK_W, GLA_QK_W, GLA_V_W, GLA_V_W, GLA_GATE_RANK, NSA_Q_W, 6 * NSA_KV_W, 3 * NSA_HEADS)
IN_WIDTH = 2 * GLA_QK_W + 2 * GLA_V_W + GLA_GATE_RANK + NSA_Q_W + 6 * NSA_KV_W + 3 * NSA_HEADS

kernel_name = 'hymba_gla_nsa_sandwich_decoder_step'

def rms_norm(x, w):
    xf = x.astype(jnp.float32)
    y = xf * lax.rsqrt(jnp.mean(xf * xf, axis=-1, keepdims=True) + EPS)
    return (y * w.astype(jnp.float32)).astype(x.dtype)

def masked_softmax(s, mask):
    s = jnp.where(mask, s.astype(jnp.float32), -1e30)
    m = jnp.max(s, axis=-1, keepdims=True)
    e = jnp.where(mask, jnp.exp(s - m), 0.0)
    return e / jnp.maximum(jnp.sum(e, axis=-1, keepdims=True), 1e-30)

def alibi_slopes():
    h = jnp.arange(1, NSA_HEADS + 1, dtype=jnp.float32)
    return (2.0 ** (-8.0 * h / NSA_HEADS)).reshape(NSA_KV_HEADS, NSA_GROUP)

def project(h, w_in, w_gla_gate, b_gla_gate):
    B, T, _ = h.shape
    z = jnp.einsum('btd,de->bte', h, w_in)
    points, acc = [], 0
    for s in IN_SIZES[:-1]:
        acc += s
        points.append(acc)
    gq, gk, gv, gr, glr, nq, nkv, ng = jnp.split(z, points, axis=-1)
    gla_q = gq.reshape(B, T, GLA_HEADS, GLA_DK) * (GLA_DK ** -0.5)
    gla_k = gk.reshape(B, T, GLA_HEADS, GLA_DK)
    gla_v = gv.reshape(B, T, GLA_HEADS, GLA_DV)
    gla_g = jax.nn.log_sigmoid((glr @ w_gla_gate + b_gla_gate).astype(jnp.float32)).reshape(B, T, GLA_HEADS, GLA_DK) / GLA_GATE_TEMP
    nsa_q = nq.reshape(B, T, NSA_KV_HEADS, NSA_GROUP, NSA_HEAD_DIM).transpose(0, 2, 3, 1, 4)
    nsa_kv = nkv.reshape(B, T, 6, NSA_KV_HEADS, NSA_HEAD_DIM)
    nsa_g = jax.nn.sigmoid(ng.astype(jnp.float32)).reshape(B, T, 3, NSA_KV_HEADS, NSA_GROUP).transpose(2, 0, 3, 4, 1)[..., None]
    return gla_q, gla_k, gla_v, gla_g, gr, nsa_q, nsa_kv, nsa_g

def gla_chunked(q, k, v, g, s0):
    B, T, H, _ = q.shape
    DV = v.shape[-1]
    C = min(GLA_CHUNK, T)
    NC = T // C

    def to_chunks(a):
        return a.astype(jnp.float32).reshape(B, NC, C, H, a.shape[-1]).transpose(1, 0, 3, 2, 4)

    causal = jnp.tril(jnp.ones((C, C), dtype=bool))

    def step(S, inp):
        qc, kc, vc, gc = inp
        b = jnp.cumsum(gc, axis=2)
        qe = qc * jnp.exp(b)
        a = jnp.where(causal, jnp.einsum('bhik,bhjk->bhij', qe, kc * jnp.exp(-b)), 0.0)
        o = jnp.einsum('bhij,bhjv->bhiv', a, vc) + jnp.einsum('bhik,bhkv->bhiv', qe, S)
        b_last = b[:, :, -1:, :]
        S = jnp.exp(b_last[:, :, 0, :, None]) * S + jnp.einsum('bhjk,bhjv->bhkv', kc * jnp.exp(b_last - b), vc)
        return S, o

    S, o = lax.scan(step, s0.astype(jnp.float32), (to_chunks(q), to_chunks(k), to_chunks(v), to_chunks(g)))
    return o.transpose(1, 0, 3, 2, 4).reshape(B, T, H, DV), S

def gla_recurrent(q, k, v, g, s0):
    def step(S, inp):
        qt, kt, vt, gt = inp
        S = jnp.exp(gt)[..., None] * S + kt[..., None] * vt[..., None, :]
        return S, jnp.einsum('bhk,bhkv->bhv', qt, S)

    seq = lambda a: a.astype(jnp.float32).transpose(1, 0, 2, 3)
    S, o = lax.scan(step, s0.astype(jnp.float32), (seq(q), seq(k), seq(v), seq(g)))
    return o.transpose(1, 0, 2, 3), S

def gla_output(o, r, gain):
    B, T = o.shape[:2]
    o = o * lax.rsqrt(jnp.mean(o * o, axis=-1, keepdims=True) + EPS) * gain.astype(jnp.float32)
    return (o.reshape(B, T, GLA_V_W) * jax.nn.silu(r.astype(jnp.float32))).astype(r.dtype)

def compress(rows, w1, pe, w2):
    B, L, Hk, Dh = rows.shape
    x = rows.transpose(0, 2, 1, 3).reshape(B * Hk, L, Dh)
    hid = lax.conv_general_dilated(x, w1.astype(x.dtype), (CMP_STRIDE,), 'VALID', dimension_numbers=('NWC', 'WIO', 'NWC'))
    hid = hid + jnp.einsum('jd,jdf->f', pe, w1).astype(hid.dtype)
    out = jax.nn.gelu(hid) @ w2
    return out.reshape(B, Hk, out.shape[1], Dh)

def cmp_attend(qg, q_pos, kc, vc, slopes):
    n = kc.shape[2]
    end = jnp.arange(n) * CMP_STRIDE + CMP_LEN - 1
    dist = (q_pos[:, None] - end[None, :]).astype(jnp.float32)
    s = jnp.einsum('bhgtd,bhnd->bhgtn', qg, kc).astype(jnp.float32) * (NSA_HEAD_DIM ** -0.5) - slopes[None, :, :, None, None] * dist
    p = masked_softmax(s, dist >= 0)
    return jnp.einsum('bhgtn,bhnd->bhgtd', p.astype(vc.dtype), vc), p

def select_blocks(p_cmp, q_pos, L):
    n_cmp = p_cmp.shape[-1]
    n_sel = -(-L // SEL_BLOCK)
    cs = jnp.arange(n_cmp) * CMP_STRIDE
    ss = jnp.arange(n_sel) * SEL_BLOCK
    overlap = ((cs[:, None] < ss[None, :] + SEL_BLOCK) & (cs[:, None] + CMP_LEN > ss[None, :])).astype(jnp.float32)
    imp = jnp.einsum('bhgtn,ns->bhts', p_cmp, overlap)
    cur = (q_pos // SEL_BLOCK)[:, None]
    j = jnp.arange(n_sel)[None, :]
    valid = j <= cur
    forced = (j == 0) | (j == cur) | (j == cur - 1)
    score = jnp.where(valid, jnp.where(forced, FORCE_SCORE, imp), NEG_SCORE)
    vals, idx = lax.top_k(score, min(SEL_TOPK, n_sel))
    return idx, vals > 0.5 * NEG_SCORE

def to_blocks(rows):
    B, L, Hk, Dh = rows.shape
    n_sel = -(-L // SEL_BLOCK)
    rows = jnp.pad(rows, ((0, 0), (0, n_sel * SEL_BLOCK - L), (0, 0), (0, 0)))
    return rows.reshape(B, n_sel, SEL_BLOCK, Hk, Dh).transpose(0, 3, 1, 2, 4)

def sel_attend(qg, q_pos, idx, ok, kb, vb, slopes):
    gather = jax.vmap(jax.vmap(lambda blocks, ix: blocks[ix]))
    kg = gather(kb, idx)
    vg = gather(vb, idx)
    pos = idx[..., None] * SEL_BLOCK + jnp.arange(SEL_BLOCK)
    dist = (q_pos[:, None, None] - pos).astype(jnp.float32)
    mask = ok[..., None] & (dist >= 0)
    s = jnp.einsum('bhgtd,bhtksd->bhgtks', qg, kg).astype(jnp.float32) * (NSA_HEAD_DIM ** -0.5) - slopes[None, :, :, None, None, None] * dist[:, :, None]
    B, Hk, G, Tq, K, SB = s.shape
    p = masked_softmax(s.reshape(B, Hk, G, Tq, K * SB), mask[:, :, None].reshape(B, Hk, 1, Tq, K * SB)).reshape(s.shape)
    return jnp.einsum('bhgtks,bhtksd->bhgtd', p.astype(vg.dtype), vg)

def win_attend(qg, q_pos, k, v, k_pos, slopes):
    dist = (q_pos[:, None] - k_pos[None, :]).astype(jnp.float32)
    mask = (k_pos[None, :] >= 0) & (dist >= 0) & (dist <= WINDOW)
    s = jnp.einsum('bhgtd,bshd->bhgts', qg, k).astype(jnp.float32) * (NSA_HEAD_DIM ** -0.5) - slopes[None, :, :, None, None] * dist
    p = masked_softmax(s, mask)
    return jnp.einsum('bhgts,bshd->bhgtd', p.astype(v.dtype), v)

def nsa_merge(g, o_cmp, o_slc, o_win, dtype):
    o = g[0] * o_cmp + g[1] * o_slc + g[2] * o_win
    B, Hk, G, T, Dh = o.shape
    return o.transpose(0, 3, 1, 2, 4).reshape(B, T, NSA_Q_W).astype(dtype)

def nsa_prompt(qg, kv, gates, cmp_k, cmp_v, slopes):
    B, Hk, G, T, Dh = qg.shape
    pos = jnp.arange(T)
    kc = compress(kv[:, :, 0], *cmp_k)
    vc = compress(kv[:, :, 1], *cmp_v)
    o_cmp, p_cmp = cmp_attend(qg, pos, kc, vc, slopes)
    idx, ok = select_blocks(p_cmp, pos, T)
    kb = to_blocks(kv[:, :, 2])
    vb = to_blocks(kv[:, :, 3])
    pad = ((0, 0), (WINDOW, 0), (0, 0), (0, 0))
    kw = jnp.pad(kv[:, :, 4], pad)
    vw = jnp.pad(kv[:, :, 5], pad)
    qb = min(NSA_QBLK, T)
    nqb = T // qb
    band = WINDOW + qb

    def blockify(a, axis):
        shape = a.shape[:axis] + (nqb, qb) + a.shape[axis + 1:]
        return jnp.moveaxis(a.reshape(shape), axis, 0)

    def one_block(args):
        n, q_blk, idx_blk, ok_blk = args
        start = n * qb
        q_pos = start + jnp.arange(qb)
        o_s = sel_attend(q_blk, q_pos, idx_blk, ok_blk, kb, vb, slopes)
        k_pos = start - WINDOW + jnp.arange(band)
        o_w = win_attend(q_blk, q_pos, lax.dynamic_slice_in_dim(kw, start, band, axis=1),
                         lax.dynamic_slice_in_dim(vw, start, band, axis=1), k_pos, slopes)
        return o_s, o_w

    o_slc, o_win = lax.map(one_block, (jnp.arange(nqb), blockify(qg, 3), blockify(idx, 2), blockify(ok, 2)))
    unblock = lambda a: jnp.moveaxis(a, 0, 3).reshape(B, Hk, G, T, Dh)
    return nsa_merge(gates, o_cmp, unblock(o_slc), unblock(o_win), qg.dtype)

def nsa_sample(qg, kv_new, gates, past, win_buf, cmp_k, cmp_v, slopes):
    B, Hk, G, Tn, Dh = qg.shape
    P = past.shape[1]
    Wb = win_buf.shape[1]
    pos = P + jnp.arange(Tn)
    rows = jnp.concatenate([past, kv_new[:, :, :4].astype(past.dtype)], axis=1)
    kc = compress(rows[:, :, 0], *cmp_k)
    vc = compress(rows[:, :, 1], *cmp_v)
    o_cmp, p_cmp = cmp_attend(qg, pos, kc, vc, slopes)
    idx, ok = select_blocks(p_cmp, pos, P + Tn)
    o_slc = sel_attend(qg, pos, idx, ok, to_blocks(rows[:, :, 2]), to_blocks(rows[:, :, 3]), slopes)
    wrows = jnp.concatenate([win_buf, kv_new[:, :, 4:].astype(win_buf.dtype)], axis=1)
    k_pos = P - Wb + jnp.arange(Wb + Tn)
    o_win = win_attend(qg, pos, wrows[:, :, 0], wrows[:, :, 1], k_pos, slopes)
    return nsa_merge(gates, o_cmp, o_slc, o_win, qg.dtype), wrows[:, -Wb:]

def finish(x, y_gla, y_nsa, w_out, norm_mix_post, norm_ffn_pre, norm_ffn_post, w_ff_up, w_ff_down):
    y = jnp.concatenate([y_gla, y_nsa], axis=-1) @ w_out
    x = x + rms_norm(y, norm_mix_post)
    h = rms_norm(x, norm_ffn_pre)
    u = jnp.square(jax.nn.relu(h @ w_ff_up))
    return x + rms_norm(u @ w_ff_down, norm_ffn_post)

def setup_inputs(seed: int = 0) -> dict:
    key = jax.random.key(seed)
    ks = jax.random.split(key, 24)
    n_pages = PAST_LEN // PAGE_SIZE
    used = DEC_BATCH * n_pages
    n_pool = used + max(1, used // 4)
    win_rows = min(WINDOW, PAST_LEN)
    f32 = jnp.float32
    nrm = lambda k, shape, scale: jax.random.normal(k, shape, f32) * scale
    gain = lambda k, n: 1.0 + 0.05 * jax.random.normal(k, (DEPTH, n), f32)
    page_table = jax.random.permutation(ks[5], n_pool)[:used].reshape(DEC_BATCH, n_pages).astype(jnp.int32)
    return {
        'x_prompt': nrm(ks[0], (BATCH, SEQ, D_MODEL), 1.0),
        'x_sample': nrm(ks[1], (DEC_BATCH, DEC_SEQ, D_MODEL), 1.0),
        'cache_nsa_kv': nrm(ks[2], (DEPTH, n_pool, PAGE_SIZE, 4, NSA_KV_HEADS, NSA_HEAD_DIM), 1.0),
        'state_nsa_win': nrm(ks[3], (DEPTH, DEC_BATCH, win_rows, 2, NSA_KV_HEADS, NSA_HEAD_DIM), 1.0),
        'state_gla': nrm(ks[4], (DEPTH, DEC_BATCH, GLA_HEADS, GLA_DK, GLA_DV), 0.5),
        'page_table': page_table,
        'norm_mix_pre': gain(ks[6], D_MODEL),
        'norm_mix_post': gain(ks[7], D_MODEL),
        'w_in': nrm(ks[8], (DEPTH, D_MODEL, IN_WIDTH), D_MODEL ** -0.5),
        'w_gla_gate': nrm(ks[9], (DEPTH, GLA_GATE_RANK, GLA_QK_W), GLA_GATE_RANK ** -0.5),
        'b_gla_gate': nrm(ks[10], (DEPTH, GLA_QK_W), 0.1),
        'gla_norm': gain(ks[11], GLA_DV),
        'w_cmpk_1': nrm(ks[12], (DEPTH, CMP_LEN, NSA_HEAD_DIM, CMP_HIDDEN), (CMP_LEN * NSA_HEAD_DIM) ** -0.5),
        'pe_cmpk': nrm(ks[13], (DEPTH, CMP_LEN, NSA_HEAD_DIM), 0.1),
        'w_cmpk_2': nrm(ks[14], (DEPTH, CMP_HIDDEN, NSA_HEAD_DIM), CMP_HIDDEN ** -0.5),
        'w_cmpv_1': nrm(ks[15], (DEPTH, CMP_LEN, NSA_HEAD_DIM, CMP_HIDDEN), (CMP_LEN * NSA_HEAD_DIM) ** -0.5),
        'pe_cmpv': nrm(ks[16], (DEPTH, CMP_LEN, NSA_HEAD_DIM), 0.1),
        'w_cmpv_2': nrm(ks[17], (DEPTH, CMP_HIDDEN, NSA_HEAD_DIM), CMP_HIDDEN ** -0.5),
        'w_out': nrm(ks[18], (DEPTH, MIX_WIDTH, D_MODEL), MIX_WIDTH ** -0.5),
        'norm_ffn_pre': gain(ks[19], D_MODEL),
        'norm_ffn_post': gain(ks[20], D_MODEL),
        'w_ff_up': nrm(ks[21], (DEPTH, D_MODEL, D_FF), D_MODEL ** -0.5),
        'w_ff_down': nrm(ks[22], (DEPTH, D_FF, D_MODEL), D_FF ** -0.5),
    }

def reference(x_prompt, x_sample, cache_nsa_kv, state_nsa_win, state_gla, page_table,
              norm_mix_pre, norm_mix_post, w_in, w_gla_gate, b_gla_gate, gla_norm,
              w_cmpk_1, pe_cmpk, w_cmpk_2, w_cmpv_1, pe_cmpv, w_cmpv_2, w_out,
              norm_ffn_pre, norm_ffn_post, w_ff_up, w_ff_down):
    slopes = alibi_slopes()
    xp, xs = x_prompt, x_sample
    Bp, T, _ = xp.shape
    Bs = xs.shape[0]
    n_pages = page_table.shape[1]
    page = cache_nsa_kv.shape[2]
    kv_p, kv_s, win_p, win_s, gla_p, gla_s = [], [], [], [], [], []
    for l in range(DEPTH):
        cmp_k = (w_cmpk_1[l], pe_cmpk[l], w_cmpk_2[l])
        cmp_v = (w_cmpv_1[l], pe_cmpv[l], w_cmpv_2[l])
        tail = (w_out[l], norm_mix_post[l], norm_ffn_pre[l], norm_ffn_post[l], w_ff_up[l], w_ff_down[l])
        h = rms_norm(xp, norm_mix_pre[l])
        gq, gk, gv, gg, gr, nq, nkv, ng = project(h, w_in[l], w_gla_gate[l], b_gla_gate[l])
        o, S = gla_chunked(gq, gk, gv, gg, jnp.zeros((Bp, GLA_HEADS, GLA_DK, GLA_DV), jnp.float32))
        y_nsa = nsa_prompt(nq, nkv, ng, cmp_k, cmp_v, slopes)
        xp = finish(xp, gla_output(o, gr, gla_norm[l]), y_nsa, *tail)
        kv_p.append(nkv[:, :, :4])
        win_p.append(nkv[:, -min(WINDOW, T):, 4:])
        gla_p.append(S)
        h = rms_norm(xs, norm_mix_pre[l])
        gq, gk, gv, gg, gr, nq, nkv, ng = project(h, w_in[l], w_gla_gate[l], b_gla_gate[l])
        o, S = gla_recurrent(gq, gk, gv, gg, state_gla[l])
        past = cache_nsa_kv[l][page_table].reshape(Bs, n_pages * page, 4, NSA_KV_HEADS, NSA_HEAD_DIM)
        y_nsa, new_win = nsa_sample(nq, nkv, ng, past, state_nsa_win[l], cmp_k, cmp_v, slopes)
        xs = finish(xs, gla_output(o, gr, gla_norm[l]), y_nsa, *tail)
        kv_s.append(nkv[:, :, :4])
        win_s.append(new_win)
        gla_s.append(S)
    return (xp, xs, jnp.stack(kv_p), jnp.stack(kv_s), jnp.stack(win_p), jnp.stack(win_s), jnp.stack(gla_p), jnp.stack(gla_s))


_drawn_inputs = setup_inputs


def setup_inputs(seed=0):
    import zlib

    import numpy as np

    out = dict(_drawn_inputs(seed))
    spreads = {}
    factors = {'pe_cmpk': 8.0}
    for name, (base, spread) in spreads.items():
        noise = np.random.default_rng([zlib.crc32(name.encode()), seed]).standard_normal(out[name].shape)
        drawn = base * np.exp(spread * noise) if base else spread * noise
        out[name] = __import__('jax').numpy.asarray(drawn.astype(out[name].dtype))
    for name, factor in factors.items():
        out[name] = (out[name] * factor).astype(out[name].dtype)
    return out
```

```python
from contextlib import ExitStack

import concourse.bass as bass
from concourse import mybir

FP32 = mybir.dt.float32
INT32 = mybir.dt.int32
ALU = mybir.AluOpType
ACT = mybir.ActivationFunctionType
AX = mybir.AxisListType
ds = bass.ds

D = 1024
T = 1024
B = 8
N = T + B
P = 128
KD = D // P
CH = N // 3
PAST = 4096
PAGE = 128
NPAGES = PAST // PAGE
WIN = 512
GH, DK, DV = 4, 64, 128
CHUNK = 64
H, KVH, HD = 8, 2, 64
G = H // KVH
CLEN, CSTR, CHID = 32, 16, 128
SELB = 64
TOPK = 16
DFF = 4096
EPS = 1e-6
MASKED = -1e30
FLOOR = -1e20
QT = T // P
C_GQ, C_GK, C_GV, C_GR = 0, 256, 512, 1024
C_GLR, C_NQ, C_KV, C_NG = 1536, 1552, 2064, 2832
RANK = 16
NGATE = 3 * H
Z_GQ, Z_GK, Z_GV, Z_GR, Z_Q, Z_KV, Z_SM = 0, 2, 4, 8, 12, 16, 22
NCP = (T - CLEN) // CSTR + 1
NCS = (PAST + 1 - CLEN) // CSTR + 1
NSELS = PAST // SELB + 1
RSEL, RWIN, RCMP = 1024, 640, 119

SAMPLE_STEPS = 20


class Chain:

    def __init__(self, eng, sem):
        self.eng, self.sem, self.base, self.k = eng, sem, 0, 0

    def enter(self, i, per):
        self.start, self.per = self.k, per
        self.base, self.k = i * per + self.k, 0

    def leave(self, rounds):
        assert self.k == self.per, (self.k, self.per)
        self.base, self.k = 0, self.start + rounds * self.per

    def mark(self, ins):
        ins.then_inc(self.sem, 1)
        self.k += 1
        return self.base + self.k

    def __call__(self, ins):
        self.eng.wait_ge(self.sem, self.mark(ins))


class Mem:
    pass


def layout(nc, ctx, M):
    def sb(name, shape, dt=FP32):
        return ctx.enter_context(nc.sbuf_tensor(name, shape, dt))

    M.xT = sb("xT", [P, KD, N])
    M.hT = sb("hT", [P, KD, N])
    M.Zf = sb("Z", [P, 24 * N])
    M.Z = M.Zf[:, :].rearrange("p (a n) -> p a n", n=N)
    M.ring = sb("ring", [P, 4096])
    M.wt = M.ring[:, :].rearrange("p (s k c) -> p s k c", s=2, c=P)
    M.srow = sb("srow", [P, 4104])
    M.misc = sb("misc", [P, 2560])
    M.ident = sb("ident", [P, P])
    M.ones = sb("ones", [P, P])
    M.nw = sb("nw", [P, 4, KD])
    M.eps = sb("eps", [P, 1])
    M.one = sb("one", [P, 1])
    M.gn = sb("gn", [P, 1])
    M.bg = sb("bg", [P, 2])
    M.wg = sb("wg", [RANK, 256])
    M.gt = sb("gt", [P, QT, NGATE])
    M.sg = sb("sg", [B, 3, B])
    M.zs = sb("zs", [P, 22, B])
    M.pn = sb("pn", [1, 2 * H])
    M.PS = ctx.enter_context(nc.psum_tensor("PS", [P, 8, 512], FP32))
    M.sems = {}

    def sem(name):
        if name not in M.sems:
            M.sems[name] = ctx.enter_context(nc.semaphore(name))
        return M.sems[name]

    M.sem = sem


def phase_load(nc, M, A, O):
    xin = M.srow[:, 0:2 * D].rearrange("p (s d) -> p s d", s=2)
    xs = M.misc[0:B, 0:D]
    x_loaded = [M.sem(f"x_loaded{s}") for s in range(2)]
    xs_loaded, gains = M.sem("xs_loaded"), M.sem("gains_loaded")
    transposed = M.sem("x_transposed")
    evac_a, evac_v = M.sem("xT_by_act"), M.sem("xT_by_dve")
    const = M.sem("const_ready")
    win_ready = [M.sem(f"win_ready{s}") for s in range(2)]
    xp = A["x_prompt"].rearrange("b (t s p) d -> (b t) s p d", s=2, p=P)
    M.NLOADS = 7

    with nc.Block() as block:
        @block.sync
        def _(sp):
            for s in range(2):
                sp.dma_start(xin[:, s, :], xp[0, s, :, :]).then_inc(x_loaded[s], 16)
            sp.dma_start(xs, A["x_sample"].rearrange("b s d -> (b s) d")).then_inc(xs_loaded, 16)
            for t in range(1, 4):
                for s in range(2):
                    sp.wait_ge(transposed, 2 * (t - 1) + s + 1)
                    sp.dma_start(xin[:, s, :], xp[t, s, :, :]).then_inc(x_loaded[s], 16)
            for s in range(2):
                sp.dma_start(M.wt[:, s, 0:KD, :],
                             A["w_in"][0, :, s * P:(s + 1) * P].rearrange("(k p) c -> p k c", p=P))\
                  .then_inc(win_ready[s], 16)

        @block.gpsimd
        def _(pool):
            c0 = M.sem("const_zeroed")
            pool.memset(M.ident[:, :], 0.0).then_inc(c0, 1)
            pool.wait_ge(c0, 1)
            pool.affine_select(out=M.ident[:, :], in_=M.ident[:, :], compare_op=ALU.not_equal, fill=1.0,
                               base=0, pattern=[[-1, P]], channel_multiplier=1).then_inc(const, 1)
            pool.memset(M.eps[:, :], EPS)
            pool.memset(M.one[:, :], 1.0)
            pool.memset(M.ones[:, :], 1.0).then_inc(const, 1)

        @block.scalar
        def _(act):
            for n, name in enumerate(("norm_mix_pre", "norm_mix_post", "norm_ffn_pre", "norm_ffn_post")):
                act.dma_start(M.nw[:, n, :], A[name].rearrange("a (k p) -> p (a k)", p=P),
                              allow_slow_non_contiguous=True).then_inc(gains, 16)
            act.dma_start(M.gn[:, :], A["gla_norm"].rearrange("a p -> p a"),
                          allow_slow_non_contiguous=True).then_inc(gains, 16)
            act.dma_start(M.bg[:, :], A["b_gla_gate"].rearrange("a (k p) -> p (a k)", p=P),
                              allow_slow_non_contiguous=True).then_inc(gains, 16)
            act.dma_start(M.wg[:, :], A["w_gla_gate"][0]).then_inc(gains, 16)
            for t in range(QT):
                s = t % 2
                act.wait_ge(transposed, t + 1)
                nc.scalar.activation(M.xT[:, 0:4, t * P:(t + 1) * P],
                                     M.PS[:, 2 * s, :].rearrange("p (k c) -> p k c", c=P), ACT.Copy)\
                  .then_inc(evac_a, 1)
            act.wait_ge(transposed, QT + 1)
            nc.scalar.activation(M.xT[:, :, T:N], M.PS[:, 4, 0:KD * B].rearrange("p (k c) -> p k c", c=B),
                                 ACT.Copy).then_inc(evac_a, 1)
            act.wait_ge(gains, 16 * M.NLOADS)

        @block.vector
        def _(dve):
            for t in range(QT):
                s = t % 2
                dve.wait_ge(transposed, t + 1)
                nc.vector.tensor_copy(M.xT[:, 4:8, t * P:(t + 1) * P],
                                      M.PS[:, 2 * s + 1, :].rearrange("p (k c) -> p k c", c=P))\
                  .then_inc(evac_v, 1)

        @block.tensor
        def _(pe):
            pe.wait_ge(const, 2)
            for t in range(QT):
                s = t % 2
                pe.wait_ge(x_loaded[s], 16 * (t // 2 + 1))
                if t >= 2:
                    pe.wait_ge(evac_a, t - 1)
                    pe.wait_ge(evac_v, t - 1)
                for k in range(KD):
                    last = nc.tensor.transpose(M.PS[:, 2 * s + k // 4, (k % 4) * P:(k % 4 + 1) * P],
                                               xin[:, s, k * P:(k + 1) * P], M.ident[:, :])
                last.then_inc(transposed, 1)
            pe.wait_ge(xs_loaded, 16)
            for k in range(KD):
                last = nc.tensor.transpose(M.PS[:, 4, k * B:(k + 1) * B], xs[:, k * P:(k + 1) * P],
                                           M.ident[0:B, 0:B])
            last.then_inc(transposed, 1)


def phase_norm(nc, M, use, src, gain, add, scratch):
    rb = M.srow[:, 0:N]
    squared, summed, logged, scale = (M.sem(f"norm_{x}") for x in ("squared", "summed", "logged", "inverse"))
    scaled = M.sem("norm_scaled")

    with nc.Block() as block:
        @block.scalar
        def _(act):
            for k in range(KD):
                nc.scalar.activation(scratch[:, k, :], src[:, k, :], ACT.Square).then_inc(squared, 1)
            act.wait_ge(summed, use + 1)
            nc.scalar.activation(rb.rearrange("p (c n) -> p c n", n=CH), M.PS[:, 0:3, 0:CH], ACT.Ln,
                                 bias=M.eps[:, 0:1], scale=1.0 / D).then_inc(logged, 1)
            act.wait_ge(logged, use + 1)
            nc.scalar.activation(rb, rb, ACT.Exp, scale=-0.5).then_inc(scale, 1)

        @block.tensor
        def _(pe):
            for k in range(KD):
                pe.wait_ge(squared, use * KD + k + 1)
                for c in range(3):
                    last = nc.tensor.matmul(M.PS[:, c, 0:CH], M.ones[:, :], scratch[:, k, c * CH:(c + 1) * CH],
                                            start=(k == 0), stop=(k == KD - 1))
            last.then_inc(summed, 1)

        @block.vector
        def _(dve):
            dve.wait_ge(scale, use + 1)
            for k in range(KD):
                nc.vector.scalar_tensor_tensor(out=(src if add else scratch)[:, k, :], in0=src[:, k, :],
                                               scalar=gain[:, k:k + 1], in1=rb, op0=ALU.mult,
                                               op1=ALU.mult).then_inc(scaled, 1)

        if add:
            @block.gpsimd
            def _(pool):
                for k in range(KD):
                    pool.wait_ge(scaled, use * KD + k + 1)
                    pool.tensor_tensor(M.xT[:, k, :], M.xT[:, k, :], src[:, k, :], ALU.add)


def dense_tile(nc, M, pe, s, kn, rhs, done):
    for k in range(kn):
        for c in range(3):
            last = nc.tensor.matmul(M.PS[:, 3 * s + c, 0:CH], M.wt[:, s, k, :], rhs(k, c),
                                    start=(k == 0), stop=(k == kn - 1))
    last.then_inc(done, 1)


def phase_project(nc, M, A):
    ready = [M.sem(f"win_ready{s}") for s in range(2)]
    done, moved = M.sem("proj_done"), M.sem("proj_moved")
    w = A["w_in"][0].rearrange("(k p) c -> p k c", p=P)

    def rhs(k, c):
        return M.hT[:, k, c * CH:(c + 1) * CH]

    def bank(s):
        return M.PS[:, 3 * s:3 * s + 3, 0:CH]

    with nc.Block() as block:
        @block.sync
        def _(sp):
            with sp.Fori(1, 6) as i:
                for s in range(2):
                    sp.wait_ge(done, 2 * i + (s - 1))
                    sp.dma_start(M.wt[:, s, 0:KD, :], w[:, :, ds(i * 256 + s * P, P)]).then_inc(ready[s], 16)
            for i in range(2):
                for s in range(2):
                    sp.wait_ge(done, 2 * (6 + i) + s - 1)
                    for half in range(2):
                        c = C_NQ + (2 * i + s + G * half) * HD
                        sp.dma_start(M.wt[:, s, 0:KD, half * HD:(half + 1) * HD], w[:, :, c:c + HD])\
                          .then_inc(ready[s], 16)
            with sp.Fori(0, 3) as i:
                for s in range(2):
                    sp.wait_ge(done, 2 * i + (16 + s - 1))
                    sp.dma_start(M.wt[:, s, 0:KD, :], w[:, :, ds(i * 256 + (C_KV + s * P), P)])\
                      .then_inc(ready[s], 16)
            sp.wait_ge(done, 21)
            sp.dma_start(M.wt[:, 0, 0:KD, 0:RANK], w[:, :, C_GLR:C_GLR + RANK]).then_inc(ready[0], 16)
            sp.dma_start(M.wt[:, 0, 0:KD, RANK:RANK + NGATE], w[:, :, C_NG:C_NG + NGATE]).then_inc(ready[0], 16)

        @block.tensor
        def _(pe):
            for s in range(2):
                pe.wait_ge(ready[s], 16)
                dense_tile(nc, M, pe, s, KD, rhs, done)
            with pe.Fori(1, 6) as i:
                for s in range(2):
                    pe.wait_ge(ready[s], 16 * i + 16)
                    pe.wait_ge(moved, 2 * i + (s - 1))
                    dense_tile(nc, M, pe, s, KD, rhs, done)
            for i in range(2):
                for s in range(2):
                    pe.wait_ge(ready[s], 16 * (6 + 2 * (i + 1)))
                    pe.wait_ge(moved, 2 * (6 + i) + s - 1)
                    dense_tile(nc, M, pe, s, KD, rhs, done)
            with pe.Fori(0, 3) as i:
                for s in range(2):
                    pe.wait_ge(ready[s], 16 * i + 16 * 11)
                    pe.wait_ge(moved, 2 * i + (16 + s - 1))
                    dense_tile(nc, M, pe, s, KD, rhs, done)
            pe.wait_ge(ready[0], 16 * 15)
            pe.wait_ge(moved, 21)
            for k in range(KD):
                for c in range(3):
                    last = nc.tensor.matmul(M.PS[0:RANK + NGATE, c, 0:CH], M.wt[:, 0, k, 0:RANK + NGATE], rhs(k, c),
                                            start=(k == 0), stop=(k == KD - 1))
            last.then_inc(done, 1)

        @block.scalar
        def _(act):
            with act.Fori(0, 11) as i:
                for s in range(2):
                    act.wait_ge(done, 2 * i + (s + 1))
                    nc.scalar.activation(M.Z[:, ds(2 * i + s, 1), :].rearrange("p a (c n) -> p (a c) n", n=CH),
                                         bank(s), ACT.Copy).then_inc(moved, 1)
            act.wait_ge(done, 23)
            nc.scalar.activation(M.Z[0:RANK + NGATE, Z_SM, :].rearrange("p (c n) -> p c n", n=CH),
                                 M.PS[0:RANK + NGATE, 0:3, 0:CH], ACT.Copy).then_inc(moved, 1)


def phase_kv_rows(nc, M, A, O):
    st = M.srow[:, 0:3 * 768].rearrange("p (s c) -> p s c", s=3)
    vtok = M.ring[:, 0:2048].rearrange("p (t b c) -> p t b c", t=QT, b=2)
    M.vtok = vtok
    turned, rows, vcop = M.sem("kv_turned"), M.sem("kv_rows"), M.sem("v_kept")
    expd, stored = M.sem("gate_exp"), [M.sem(f"rows_stored{s}") for s in range(3)]
    wmove, sgl, onep = M.sem("win_moved"), M.sem("sg_loaded"), M.sem("gate_onep")
    sgate = M.sem("sg_exp")
    kvp = O["kv_prompt"].rearrange("a b (t p) c k d -> (a b t) p (c k d)", p=P)
    wnp = O["win_prompt"].rearrange("a b (t p) c k d -> (a b t) p (c k d)", p=P)

    def stores_of_slot(t):
        return sum(1 + (u >= QT - WIN // P) for u in range(t % 2, t + 1, 2))

    with nc.Block() as block:
        @block.tensor
        def _(pe):
            for t in range(QT + 1):
                s, n = t % 2, (P if t < QT else B)
                if t >= 2:
                    pe.wait_ge(rows, t - 1)
                for j in range(6):
                    nc.tensor.transpose(M.PS[0:n, 2 * s + j // 4, (j % 4) * P:(j % 4 + 1) * P],
                                        M.Z[:, Z_KV + j, t * P:t * P + n], M.ident[:, :])\
                      .then_inc(turned, 1)
                if t < QT:
                    nc.tensor.transpose(M.PS[:, 2 * s + 1, 256:256 + 40], M.Z[0:40, Z_SM, t * P:t * P + n],
                                        M.ident[0:40, 0:40]).then_inc(turned, 1)

        @block.scalar
        def _(act):
            act.dma_start(O["win_sample"][0, :, 0:WIN - 1].rearrange("b r c k d -> b (r c k d)"),
                          A["state_nsa_win"][0, :, 1:WIN].rearrange("b r c k d -> b (r c k d)")).then_inc(wmove, 16)
            for br in range(3):
                act.dma_start(M.sg[:, br, :], M.Z[RANK + br * H:RANK + (br + 1) * H, Z_SM, T:N]).then_inc(sgl, 16)
            for t in range(QT + 1):
                s, n = t % 2, (P if t < QT else B)
                act.wait_ge(turned, 7 * t + (7 if t < QT else 6))
                if t >= 2:
                    act.wait_ge(stored[s], 16 * stores_of_slot(t - 2))
                    act.wait_ge(vcop, t - 1)
                if t < QT:
                    nc.scalar.activation(M.gt[:, t, :], M.PS[:, 2 * s + 1, 256 + RANK:256 + 40], ACT.Exp,
                                         scale=-1.0).then_inc(expd, 1)
                nc.scalar.activation(st[0:n, s, 0:512], M.PS[0:n, 2 * s, :], ACT.Copy)
                nc.scalar.activation(st[0:n, s, 512:768], M.PS[0:n, 2 * s + 1, 0:256], ACT.Copy)\
                  .then_inc(rows, 1)
            act.wait_ge(sgl, 48)
            nc.scalar.activation(M.sg[:, :, :], M.sg[:, :, :], ACT.Exp, scale=-1.0).then_inc(sgate, 1)
            act.wait_ge(wmove, 16)

        @block.gpsimd
        def _(pool):
            for t in range(QT):
                s = t % 2
                pool.wait_ge(rows, t + 1)
                pool.tensor_copy(vtok[:, t, 0, :], st[:, s, 384:512])
                pool.tensor_copy(vtok[:, t, 1, :], st[:, s, 640:768]).then_inc(vcop, 1)
            pool.tensor_copy(M.zs[:, :, :], M.Z[:, 0:22, T:N]).then_inc(vcop, 1)

        @block.vector
        def _(dve):
            dve.wait_ge(expd, QT)
            for buf, sem in ((M.gt, expd), (M.sg, sgate)):
                if buf is M.sg:
                    dve.wait_ge(sgate, 1)
                nc.vector.tensor_scalar_add(buf[:, :, :], buf[:, :, :], 1.0).then_inc(onep, 1)
                dve.wait_ge(onep, 1 if buf is M.gt else 2)
                nc.vector.reciprocal(buf[:, :, :], buf[:, :, :])

        @block.sync
        def _(sp):
            for t in range(QT):
                s = t % 2
                sp.wait_ge(rows, t + 1)
                sp.dma_start(kvp[t], st[:, s, 0:512]).then_inc(stored[s], 16)
                if t >= QT - WIN // P:
                    sp.dma_start(wnp[t - (QT - WIN // P)], st[:, s, 512:768]).then_inc(stored[s], 16)
            sp.wait_ge(rows, QT + 1)
            sp.dma_start(O["kv_sample"].rearrange("a b s c k d -> (a b s) (c k d)"), st[0:B, 0, 0:512])\
              .then_inc(stored[0], 16)
            sp.dma_start(O["win_sample"][0, :, WIN - 1].rearrange("b c k d -> b (c k d)"), st[0:B, 0, 512:768])\
              .then_inc(stored[0], 16)
            sp.wait_ge(stored[0], 16 * 8)
            sp.wait_ge(stored[1], 16 * 6)


def phase_gla(nc, M, A, O):
    gT = M.srow[:, 0:2 * N].rearrange("p (a n) -> p a n", a=2)
    soft = [M.Z[:, 23, :], M.srow[:, 2 * N:3 * N]]
    tri = M.ring[:, 2048:2048 + P]

    def pair(base, buf=M.misc, n=2):
        return buf[:, base:base + n * P].rearrange("p (a n) -> p a n", a=n)

    bt, eb, enb, dl = pair(0), pair(256), pair(512), pair(768)
    qe, ke, kl = pair(1024), pair(1280), pair(1536)
    Sa, Sb = pair(1792), pair(2048)
    eg = M.misc[:, 2304:2320].rearrange("p (b a) -> p b a", a=2)
    qs = M.misc[:, 2320:2336].rearrange("p (a b) -> p a b", a=2)
    v_s, vtk = pair(2064, M.srow, 4), pair(2576, M.srow, 4)
    kltk, Am = pair(3088, M.srow), pair(3344, M.srow, 4)
    Amq = Am.rearrange("p (q a) n -> p q a n", q=2)
    state = M.srow[:, 0:2 * B * DV].rearrange("p (b a v) -> p b a v", b=B, a=2)
    dg = pair(2064, M.srow, 4)
    X, Y, OB, DS, VT, KT = 0, 1, 2, 4, 6, 7
    EXP = ACT.Exp
    S = M.sem
    xg, absd, soft_r, g_ready = S("gate_x"), S("gate_abs"), S("gate_soft"), S("gate_ready")
    step = S("gla_dve_step")
    scan, dlr, ebr, edl = S("scan_ready"), S("dl_ready"), S("eb_ready"), S("edl_ready")
    qk, klr, vst, vtd, ktd = S("qk_ready"), S("kl_ready"), S("v_static"), S("v_turned"), S("kl_turned")
    vke, ar, amr, dsr, in0 = S("vk_rows"), S("a_ready"), S("am_ready"), S("ds_ready"), S("inter0")
    sbr, sar, orr, oev = S("sb_ready"), S("sa_ready"), S("o_ready"), S("o_moved")
    tri_r, st_l, egr, dgr, vb = S("tri_ready"), S("state_loaded"), S("eg_ready"), S("dg_ready"), S("vb_ready")
    stn, so, stored, soe, qsr = S("state_new"), S("so_ready"), S("gla_stored"), S("so_moved"), S("qs_ready")
    sq, ss, rt, den, rs, mixed = S("o_sq"), S("o_ss"), S("o_root"), S("o_exp"), S("o_scaled"), S("o_mixed")

    with nc.Block() as block:
        @block.gpsimd
        def _(pool):
            t0 = S("tri_steps")
            pool.memset(tri, 1.0).then_inc(t0, 1)
            pool.wait_ge(t0, 1)
            pool.affine_select(out=tri, in_=tri, compare_op=ALU.is_ge, fill=0.0, base=0,
                               pattern=[[1, P]], channel_multiplier=-1).then_inc(t0, 1)
            pool.wait_ge(t0, 2)
            pool.affine_select(out=tri[:, CHUNK:P], in_=tri[:, CHUNK:P], compare_op=ALU.is_ge, fill=0.0,
                               base=-CHUNK, pattern=[[0, CHUNK]], channel_multiplier=1).then_inc(tri_r, 1)
            pool.wait_ge(g_ready, 2)
            with pool.Fori(0, QT) as t:
                pool.wait_ge(vtd, t + 1)
                pool.tensor_copy(v_s, M.Z[:, Z_GV:Z_GV + 4, ds(t * P, P)]).then_inc(vst, 1)

        @block.scalar
        def _(act):
            for a in range(2):
                act.wait_ge(xg, a + 1)
                nc.scalar.activation(soft[a].rearrange("p (c n) -> p c n", n=CH), M.PS[:, 3 * a:3 * a + 3, 0:CH],
                                     ACT.Abs, bias=M.bg[:, a:a + 1]).then_inc(absd, 1)
            act.wait_ge(absd, 2)
            for a in range(2):
                nc.scalar.activation(soft[a], soft[a], EXP, scale=-1.0).then_inc(soft_r, 1)
            act.wait_ge(soft_r, 2)
            for a in range(2):
                nc.scalar.activation(soft[a], soft[a], ACT.Ln, bias=M.one[:, 0:1]).then_inc(soft_r, 1)
            act.wait_ge(g_ready, 2)
            nc.scalar.activation(eg.rearrange("p b a -> p a b"), gT[:, :, T:N], EXP, scale=1 / 16).then_inc(egr, 1)
            with act.Fori(0, QT) as t:
                act.wait_ge(scan, t + 1)
                nc.scalar.activation(eb, bt, EXP, scale=1 / 16)
                nc.scalar.activation(enb, bt, EXP, scale=-1 / 16).then_inc(ebr, 1)
                act.wait_ge(dlr, t + 1)
                nc.scalar.activation(dl, dl, EXP, scale=1 / 16).then_inc(edl, 1)
                act.wait_ge(orr, t + 1)
                act.wait_ge(vtd, t + 2)
                nc.scalar.activation(vtk, M.PS[:, VT, :].rearrange("p (a n) -> p a n", n=P), ACT.Copy)
                act.wait_ge(ktd, t + 1)
                nc.scalar.activation(kltk, M.PS[:, KT, 0:256].rearrange("p (a n) -> p a n", n=P), ACT.Copy)\
                  .then_inc(vke, 1)
                act.wait_ge(orr, t + 2)
                for q in range(2):
                    last = nc.scalar.activation(M.hT[:, q:4:2, ds(t * P, P)],
                                                M.PS[:, OB + q, 0:256].rearrange("p (a n) -> p a n", n=P), ACT.Copy)
                last.then_inc(oev, 1)
            for h in range(GH):
                nc.scalar.activation(M.Z[:, 4 + h, :], M.Z[:, Z_GR + h, :], ACT.Sigmoid).then_inc(den, 1)
            act.wait_ge(so, 1)
            for q in range(2):
                nc.scalar.activation(M.hT[:, q:4:2, T:N], M.PS[:, OB + q, 0:16].rearrange("p (a b) -> p a b", b=B),
                                     ACT.Copy).then_inc(soe, 1)
            act.wait_ge(soe, 2)
            for h in range(GH):
                nc.scalar.activation(M.Z[:, h, :], M.hT[:, h, :], ACT.Square).then_inc(sq, 1)
            for h in range(GH):
                act.wait_ge(ss, h + 1)
                nc.scalar.activation(M.Z[:, h, :].rearrange("p (c n) -> p c n", n=CH),
                                     M.PS[:, 3 * (h % 2):3 * (h % 2) + 3, 0:CH], ACT.Ln,
                                     bias=M.eps[:, 0:1], scale=1.0 / DV).then_inc(rt, 1)
            for h in range(GH):
                act.wait_ge(rt, h + 1)
                nc.scalar.activation(M.Z[:, h, :], M.Z[:, h, :], EXP, scale=-0.5).then_inc(rs, 1)

        @block.vector
        def _(dve):
            ch = Chain(dve, step)
            dve.wait_ge(absd, 2)
            for a in range(2):
                ch(nc.vector.tensor_scalar(gT[:, a, :].rearrange("p (c n) -> p c n", n=CH),
                                           M.PS[:, 3 * a:3 * a + 3, 0:CH], M.bg[:, a:a + 1], 0.0,
                                           ALU.add, ALU.min))
            for a in range(2):
                dve.wait_ge(soft_r, 3 + a)
                nc.vector.tensor_tensor(gT[:, a, :], gT[:, a, :], soft[a], ALU.subtract).then_inc(g_ready, 1)
            nc.vector.tensor_scalar_mul(qs, M.zs[:, Z_GQ:Z_GQ + 2, :], DK ** -0.5).then_inc(qsr, 1)
            ch(nc.vector.memset(Sa, 0.0))
            dve.wait_ge(g_ready, 2)
            dve.wait_ge(tri_r, 1)
            with dve.Fori(0, QT) as t:
                for a in range(2):
                    for c in range(2):
                        last = nc.vector.tensor_tensor_scan(
                            bt[:, a, c * CHUNK:(c + 1) * CHUNK], M.ones[:, 0:CHUNK],
                            gT[:, a, ds(t * P + c * CHUNK, CHUNK)], 0.0, ALU.mult, ALU.add)
                last.then_inc(scan, 1)
                dve.wait_ge(scan, t + 1)
                b4 = bt.rearrange("p a (c n) -> p (a c) n", n=CHUNK)
                ends = b4[:, :, CHUNK - 1:CHUNK].to_broadcast([P, 4, CHUNK])
                nc.vector.tensor_tensor(dl.rearrange("p a (c n) -> p (a c) n", n=CHUNK), ends, b4, ALU.subtract)\
                  .then_inc(dlr, 1)
                dve.wait_ge(ebr, t + 1)
                dve.wait_ge(orr, t + 1)
                nc.vector.scalar_tensor_tensor(out=qe, in0=M.Z[:, Z_GQ:Z_GQ + 2, ds(t * P, P)], scalar=DK ** -0.5,
                                               in1=eb, op0=ALU.mult, op1=ALU.mult)
                nc.vector.tensor_tensor(ke, M.Z[:, Z_GK:Z_GK + 2, ds(t * P, P)], enb, ALU.mult).then_inc(qk, 1)
                dve.wait_ge(edl, t + 1)
                nc.vector.tensor_tensor(kl, M.Z[:, Z_GK:Z_GK + 2, ds(t * P, P)], dl, ALU.mult).then_inc(klr, 1)
                dve.wait_ge(ar, t + 1)
                for q in range(2):
                    last = nc.vector.tensor_tensor(Amq[:, q, :, :],
                                                   M.PS[:, X + q, 0:256].rearrange("p (a n) -> p a n", n=P),
                                                   tri.rearrange("p (a n) -> p a n", a=1).to_broadcast([P, 2, P]),
                                                   ALU.mult)
                last.then_inc(amr, 1)
                dve.wait_ge(dsr, t + 1)
                for a in range(2):
                    last = nc.vector.scalar_tensor_tensor(
                        out=Sb[:, a, :], in0=Sa[:, a, :], scalar=eb[:, a, CHUNK - 1:CHUNK],
                        in1=M.PS[:, DS, a * P:(a + 1) * P], op0=ALU.mult, op1=ALU.add)
                last.then_inc(sbr, 1)
                dve.wait_ge(sbr, t + 1)
                dve.wait_ge(in0, t + 1)
                for a in range(2):
                    last = nc.vector.scalar_tensor_tensor(
                        out=Sa[:, a, :], in0=Sb[:, a, :], scalar=eb[:, a, P - 1:P],
                        in1=M.PS[:, DS + 1, a * P:(a + 1) * P], op0=ALU.mult, op1=ALU.add)
                last.then_inc(sar, 1)
                dve.wait_ge(sar, t + 1)
            dve.wait_ge(st_l, 16)
            dve.wait_ge(egr, 1)
            ch(nc.vector.tensor_tensor(state.rearrange("p b a v -> p (b a) v"), state.rearrange("p b a v -> p (b a) v"),
                                       eg.rearrange("p b a -> p (b a)").rearrange("p (x y) -> p x y", y=1)
                                       .to_broadcast([P, 2 * B, DV]), ALU.mult))
            for b in range(B):
                if b >= 1:
                    dve.wait_ge(vb, b)
                nc.vector.tensor_tensor(dg, M.ident[:, :].rearrange("p (a n) -> p a n", a=1).to_broadcast([P, 4, P]),
                                        M.zs[:, Z_GV:Z_GV + 4, b:b + 1].to_broadcast([P, 4, P]), ALU.mult)\
                  .then_inc(dgr, 1)
                dve.wait_ge(vb, b + 1)
                for a in range(2):
                    last = nc.vector.scalar_tensor_tensor(out=state[:, b, a, :],
                                                          in0=M.PS[:, X + b % 2, a * P:(a + 1) * P],
                                                          scalar=M.zs[:, Z_GK + a, b:b + 1], in1=state[:, b, a, :],
                                                          op0=ALU.mult, op1=ALU.add)
                last.then_inc(stn, 1)
            for h in range(GH):
                t1 = M.Z[:, 4 + h, :]
                dve.wait_ge(den, h + 1)
                ch(nc.vector.tensor_tensor(t1, t1, M.Z[:, Z_GR + h, :], ALU.mult))
                dve.wait_ge(rs, h + 1)
                ch(nc.vector.scalar_tensor_tensor(out=M.Z[:, h, :], in0=M.Z[:, h, :], scalar=M.gn[:, 0:1],
                                                  in1=t1, op0=ALU.mult, op1=ALU.mult))
                nc.vector.tensor_tensor(M.hT[:, h, :], M.hT[:, h, :], M.Z[:, h, :], ALU.mult).then_inc(mixed, 1)

        @block.tensor
        def _(pe):
            for a in range(2):
                for c in range(3):
                    last = nc.tensor.matmul(M.PS[:, 3 * a + c, 0:CH], M.wg[:, a * P:(a + 1) * P],
                                            M.Z[0:RANK, Z_SM, c * CH:(c + 1) * CH], start=True, stop=True)
                last.then_inc(xg, 1)
            pe.sem_inc(vtd, 1)
            pe.sem_inc(orr, 1)
            with pe.Fori(0, QT) as t:
                pe.wait_ge(vst, t + 1)
                for h in range(GH):
                    last = nc.tensor.transpose(M.PS[:, VT, h * P:(h + 1) * P], v_s[:, h, :], M.ident[:, :])
                last.then_inc(vtd, 1)
                pe.wait_ge(qk, t + 1)
                for a in range(2):
                    for q in range(2):
                        r = slice(q * DK, (q + 1) * DK)
                        last = nc.tensor.matmul(M.PS[:, X + q, a * P:(a + 1) * P], ke[r, a, :], qe[r, a, :],
                                                start=True, stop=True)
                last.then_inc(ar, 1)
                pe.wait_ge(klr, t + 1)
                for a in range(2):
                    last = nc.tensor.transpose(M.PS[:, KT, a * P:(a + 1) * P], kl[:, a, :], M.ident[:, :])
                last.then_inc(ktd, 1)
                pe.wait_ge(vke, t + 1)
                pe.wait_ge(amr, t + 1)
                for a in range(2):
                    for q in range(2):
                        nc.tensor.matmul(M.PS[:, OB + q, a * P:(a + 1) * P], vtk[:, 2 * a + q, :],
                                         Amq[:, q, a, :], start=(a == 0), stop=False, skip_group_check=True)
                for c in range(2):
                    for a in range(2):
                        for q in range(2):
                            last = nc.tensor.matmul(M.PS[q * DK:(q + 1) * DK, DS + c, a * P:(a + 1) * P],
                                                    kltk[c * CHUNK:(c + 1) * CHUNK, a, q * DK:(q + 1) * DK],
                                                    vtk[c * CHUNK:(c + 1) * CHUNK, 2 * a + q, :],
                                                    start=True, stop=True)
                last.then_inc(dsr, 1)

                def inter(state_, c):
                    for a in range(2):
                        for q in range(2):
                            r = slice(q * DK, (q + 1) * DK)
                            last = nc.tensor.matmul(M.PS[:, OB + q, a * P + c * CHUNK:a * P + (c + 1) * CHUNK],
                                                    state_[r, a, :], qe[r, a, c * CHUNK:(c + 1) * CHUNK],
                                                    start=False, stop=True, skip_group_check=True)
                    return last

                inter(Sa, 0).then_inc(in0, 1)
                pe.wait_ge(sbr, t + 1)
                inter(Sb, 1).then_inc(orr, 1)
            for b in range(B):
                pe.wait_ge(dgr, b + 1)
                if b >= 2:
                    pe.wait_ge(stn, b - 1)
                for q in range(2):
                    last = nc.tensor.matmul(M.PS[q * DK:(q + 1) * DK, X + b % 2, 0:256], M.ones[:, 0:DK],
                                            dg[:, q:4:2, :], start=True, stop=True)
                last.then_inc(vb, 1)
            pe.wait_ge(stn, B)
            pe.wait_ge(qsr, 1)
            pe.wait_ge(oev, QT)
            for b in range(B):
                for a in range(2):
                    for q in range(2):
                        r = slice(q * DK, (q + 1) * DK)
                        last = nc.tensor.matmul(M.PS[:, OB + q, a * B + b:a * B + b + 1], state[r, b, a, :],
                                                qs[r, a, b:b + 1], start=True, stop=True)
            last.then_inc(so, 1)
            for h in range(GH):
                pe.wait_ge(sq, h + 1)
                if h >= 2:
                    pe.wait_ge(rt, h - 1)
                for c in range(3):
                    last = nc.tensor.matmul(M.PS[:, 3 * (h % 2) + c, 0:CH], M.ones[:, :],
                                            M.Z[:, h, c * CH:(c + 1) * CH], start=True, stop=True)
                last.then_inc(ss, 1)

        @block.sync
        def _(sp):
            sp.wait_ge(sar, QT)
            sp.dma_start(O["gla_prompt"][0, 0].rearrange("(a q) k v -> (q k) a v", q=2), Sa).then_inc(stored, 16)
            sp.dma_start(state, A["state_gla"][0].rearrange("b (a q) k v -> (q k) b a v", q=2)).then_inc(st_l, 16)
            sp.wait_ge(stn, B)
            sp.dma_start(O["gla_sample"][0].rearrange("b (a q) k v -> (q k) b a v", q=2), state).then_inc(stored, 16)
            sp.wait_ge(stored, 32)


def phase_compress(nc, M, A):
    M.w1 = M.Zf[:, 0:4096].rearrange("p (v j f) -> p v j f", v=2, f=CHID)
    M.pe = M.misc[:, 192:224].rearrange("p (v j) -> p v j", v=2)
    M.w2 = M.misc[:, 224:352].rearrange("p (v d) -> p v d", v=2)
    M.hb = M.misc[:, 604:606]
    M.kcT, M.vcp = M.misc[:, 0:NCP], M.misc[:, 64:64 + P]
    hid = M.misc[:, 352:352 + 4 * NCP].rearrange("p (v h n) -> p v h n", v=2, h=2)
    x2 = M.Zf[:, 8576:8576 + 2048].rearrange("p (v h r n) -> p v h r n", v=2, h=2, r=8)
    M.slope = M.misc[:, 608:616].rearrange("p (k g) -> p k g", k=KVH)
    RS, RW, RC = M.srow[:, 0:RSEL], M.srow[:, RSEL:RSEL + RWIN], M.srow[:, RSEL + RWIN:RSEL + RWIN + RCMP]
    w_l, x2_r, conv, hidr, kv_r = (M.sem(x) for x in ("cmp_w_loaded", "cmp_x", "cmp_conv", "cmp_hid", "cmp_kv"))
    tm, hbr, slr = M.sem("template_step"), M.sem("cmp_bias"), M.sem("slopes_set")

    with nc.Block() as block:
        @block.sync
        def _(sp):
            for v, (w1, pe_, w2) in enumerate((("w_cmpk_1", "pe_cmpk", "w_cmpk_2"), ("w_cmpv_1", "pe_cmpv", "w_cmpv_2"))):
                sp.dma_start(M.w1[:, v, :, :], A[w1][0].rearrange("(j q) d f -> (q d) j f", q=2)).then_inc(w_l, 16)
                sp.dma_start(M.pe[:, v, :], A[pe_][0].rearrange("(j q) d -> (q d) j", q=2),
                             allow_slow_non_contiguous=True).then_inc(w_l, 16)
                sp.dma_start(M.w2[:, v, :], A[w2][0]).then_inc(w_l, 16)

        @block.gpsimd
        def _(pool):
            for h in range(H):
                pool.memset(M.slope[:, h // G, h % G:h % G + 1], 2.0 ** (-8.0 * (h + 1) / H)).then_inc(slr, 1)
            for r, pat, base in ((RS, [[1, RSEL]], -(T - P)), (RW, [[1, RWIN]], -WIN),
                                 (RC, [[CSTR, RCMP]], CLEN - 1 - (T - P))):
                pool.iota(r, pattern=pat, base=base, channel_multiplier=-1,
                          allow_small_or_imprecise_dtypes=True).then_inc(tm, 1)
            pool.wait_ge(tm, 3)
            for r, pat, base in ((RS, [[-1, RSEL]], T - P), (RW, [[-1, RWIN]], WIN),
                                 (RC, [[-CSTR, RCMP]], T - P - (CLEN - 1))):
                pool.affine_select(out=r, in_=r, compare_op=ALU.is_ge, fill=MASKED, base=base, pattern=pat,
                                   channel_multiplier=1).then_inc(tm, 1)
            pool.wait_ge(tm, 6)
            pool.affine_select(out=RW, in_=RW, compare_op=ALU.is_ge, fill=MASKED, base=0, pattern=[[1, RWIN]],
                               channel_multiplier=-1).then_inc(tm, 1)

        @block.vector
        def _(dve):
            for v in range(2):
                for h in range(2):
                    for q in range(2):
                        src = M.Z[h * HD:(h + 1) * HD, Z_KV + v, 0:T].rearrange("p (n r q) -> p q r n", r=8, q=2)
                        last = nc.vector.tensor_copy(x2[q * HD:(q + 1) * HD, v, h, :, :], src[:, q, :, :])
                last.then_inc(x2_r, 1)

        @block.tensor
        def _(pe):
            pe.wait_ge(w_l, 96)
            for v in range(2):
                for j in range(16):
                    last = nc.tensor.matmul(M.PS[:, 2 + v, 0:1], M.w1[:, v, j, :], M.pe[:, v, j:j + 1],
                                            start=(j == 0), stop=(j == 15))
            last.then_inc(conv, 1)
            for v in range(2):
                pe.wait_ge(x2_r, v + 1)
                for j in range(16):
                    last = nc.tensor.matmul(M.PS[:, v, 0:2 * NCP], M.w1[:, v, j, :],
                                            x2[:, v, :, j % 8, j // 8:j // 8 + NCP], start=(j == 0), stop=(j == 15))
                last.then_inc(conv, 1)
            pe.wait_ge(hidr, 2)
            for h in range(2):
                nc.tensor.matmul(M.PS[h * HD:(h + 1) * HD, 4, 0:NCP], M.w2[:, 0, :], hid[:, 0, h, :],
                                 start=True, stop=True)
            for h in range(2):
                last = nc.tensor.matmul(M.PS[0:NCP, 5, h * HD:(h + 1) * HD], hid[:, 1, h, :], M.w2[:, 1, :],
                                        start=True, stop=True)
            last.then_inc(kv_r, 1)

        @block.scalar
        def _(act):
            act.wait_ge(conv, 1)
            nc.scalar.activation(M.hb, M.PS[:, 2:4, 0], ACT.Copy).then_inc(hbr, 1)
            act.wait_ge(hbr, 1)
            for v in range(2):
                act.wait_ge(conv, v + 2)
                nc.scalar.activation(hid[:, v, :, :].rearrange("p h n -> p (h n)"), M.PS[:, v, 0:2 * NCP],
                                     ACT.Gelu_apprx_tanh, bias=M.hb[:, v:v + 1]).then_inc(hidr, 1)
            act.wait_ge(kv_r, 1)
            nc.scalar.activation(M.kcT, M.PS[:, 4, 0:NCP], ACT.Copy)
            nc.scalar.activation(M.vcp[0:NCP, :], M.PS[0:NCP, 5, 0:P], ACT.Copy)


def phase_attend(nc, M):
    RT = RSEL + RWIN + RCMP
    q_s = M.Zf[:, 4096:4096 + T]
    W = T + RWIN + 64
    sbuf = M.Zf[:, 5120:5120 + 2 * W].rearrange("p (s w) -> p s w", s=2)
    pt = M.Zf[:, 8576:8576 + 2 * 14 * P].rearrange("p (s w) -> p s w", s=2)
    RB = [M.srow[:, RT:2 * RT], M.ring[:, 2048:2048 + RT]]
    ytok = M.misc[:, 616:616 + 2 * P].rearrange("p (s c) -> p s c", s=2)
    neg = M.misc[:, 880:888].rearrange("p (s c) -> p s c", s=2)
    mx = M.misc[:, 888:896].rearrange("p (s c) -> p s c", s=2)
    sm = M.misc[:, 896:904].rearrange("p (s c) -> p s c", s=2)
    rc = M.misc[:, 904:912].rearrange("p (s c) -> p s c", s=2)
    PSf = M.PS[:, :, :].rearrange("p b n -> p (b n)")
    CMP0, WIN0, SEL0 = T + RWIN, T, 0
    U = 2 * QT

    def shape(u):
        qt, kvh = u // 2, u % 2
        j0 = max(0, qt - WIN // P)
        return qt, kvh, j0, (qt + 1) * P, (qt - j0 + 1) * P

    def tiles(u):
        qt, _, j0, ls, lw = shape(u)
        t = [(WIN0 + c, P) for c in range(0, lw, P)] + [(SEL0 + c, P) for c in range(0, ls, P)]
        return t[:3] + [(CMP0, NCP)] + t[3:]

    def groups(u):
        t = tiles(u)
        return [t[g:g + 4] for g in range(0, len(t), 4)]

    first = [sum(len(groups(v)) for v in range(u)) for u in range(U + 1)]
    NG = first[U]
    assert NG % 2 == 0
    q_r, rb_r = M.sem("q_slot"), M.sem("rb_ready")
    scores, sread, maxr, probs = M.sem("scores"), M.sem("scores_read"), M.sem("max_ready"), M.sem("probs")
    turned, ptm, pv, merged = M.sem("p_turned"), M.sem("p_moved"), M.sem("pv_done"), M.sem("merged")
    yt, ym, step = M.sem("y_turned"), M.sem("y_moved"), M.sem("merge_step")
    passed = M.sem("attend_passed")
    per = 7 * U

    with nc.Block() as block:
        @block.gpsimd
        def _(pool):
            with pool.Fori(0, G) as hh:
                pool.wait_ge(sread, hh * U + 1)
                for kvh in range(KVH):
                    last = pool.tensor_tensor(RB[kvh], M.srow[:, 0:RT],
                                              M.slope[:, kvh, ds(hh, 1)].to_broadcast([P, RT]), ALU.mult)
                last.then_inc(rb_r, 1)

        @block.scalar
        def _(act):
            def exps(hh, u):
                qt, kvh, j0, ls, lw = shape(u)
                s = u % 2
                act.wait_ge(maxr, hh * U + (u + 1))
                for br, (c, w) in enumerate(((CMP0, NCP), (SEL0, ls), (WIN0, lw))):
                    last = nc.scalar.activation(sbuf[:, s, c:c + w], sbuf[:, s, c:c + w], ACT.Exp,
                                                bias=neg[:, s, br:br + 1], accum_out=sm[:, s, br:br + 1])
                last.then_inc(probs, 1)

            def y_out(hh, qt):
                act.wait_ge(yt, hh * QT + (qt + 1))
                nc.scalar.activation(M.hT[:, ds(hh + 4, 1), qt * P:(qt + 1) * P],
                                     M.PS[:, 7:8, 256:384], ACT.Copy).then_inc(ym, 1)

            with act.Fori(0, G) as hh:
                nc.scalar.activation(q_s, M.Z[:, ds(hh + Z_Q, 1), 0:T].rearrange("p a n -> p (a n)"), ACT.Copy,
                                     scale=HD ** -0.5).then_inc(q_r, 1)
                exps(hh, 0)
                for u in range(U):
                    for g, grp in enumerate(groups(u)):
                        act.wait_ge(turned, hh * NG + (first[u] + g + 1))
                        if g == 0:
                            act.wait_ge(pv, hh * U + (u + 1))
                        o, bank = g * 4 * P, M.PS[:, 4 + (first[u] + g) % 2, :]
                        n = (len(grp) - (g == 0)) * P
                        last = nc.scalar.activation(pt[:, u % 2, o:o + n], bank[:, 0:n], ACT.Copy)
                        if g == 0:
                            last = nc.scalar.activation(pt[0:NCP, u % 2, n:n + P], bank[0:NCP, n:n + P], ACT.Copy)
                        last.then_inc(ptm, 1)
                    if u + 1 < U:
                        exps(hh, u + 1)
                    if u % 2 == 0 and u >= 2:
                        y_out(hh, u // 2 - 1)
                y_out(hh, QT - 1)

        @block.vector
        def _(dve):
            ch = Chain(dve, step)
            dve.sem_inc(sread, 1)
            dve.sem_inc(merged, 2)

            def score(hh, u):
                qt, kvh, j0, ls, lw = shape(u)
                s = u % 2
                dve.wait_ge(scores, hh * U + (u + 1))
                if u >= 2:
                    dve.wait_ge(turned, hh * NG + first[u - 1])
                offs = ((CMP0, NCP, RSEL + RWIN + (T - P) // CSTR - qt * P // CSTR), (SEL0, ls, T - P - qt * P),
                        (WIN0, lw, RSEL + (j0 - qt) * P + WIN))
                dve.sem_inc(passed, 1)
                for br, (c, w, r) in enumerate(offs):
                    last = nc.vector.tensor_tensor_reduce(out=sbuf[:, s, c:c + w], in0=PSf[:, c:c + w],
                                                          in1=RB[kvh][:, r:r + w], scale=1.0, scalar=FLOOR,
                                                          op0=ALU.add, op1=ALU.max, accum_out=mx[:, s, br:br + 1])
                last.then_inc(sread, 1)
                dve.wait_ge(sread, hh * U + (u + 2))
                nc.vector.tensor_scalar_mul(neg[:, s, 0:3], mx[:, s, 0:3], -1.0).then_inc(maxr, 1)

            def merge(hh, u):
                qt, kvh = u // 2, u % 2
                s = u % 2
                dve.wait_ge(probs, hh * U + (u + 1))
                ch(nc.vector.tensor_scalar_max(rc[:, s, 0:3], sm[:, s, 0:3], 1e-30))
                ch(nc.vector.reciprocal(rc[:, s, 0:3], rc[:, s, 0:3]))
                gates = M.gt[:, qt, :].rearrange("p (b h) -> p b h", b=3)[:, :, ds(hh + G * kvh, 1)]
                ch(nc.vector.tensor_tensor(rc[:, s, 0:3].rearrange("p (b h) -> p b h", h=1),
                                           rc[:, s, 0:3].rearrange("p (b h) -> p b h", h=1), gates, ALU.mult))
                dve.wait_ge(pv, hh * U + (u + 3))
                y = ytok[:, qt % 2, kvh * HD:(kvh + 1) * HD]
                if kvh == 0 and qt >= 2:
                    dve.wait_ge(yt, hh * QT + (qt - 1))
                o = M.PS[:, 6 + kvh, 0:3 * HD].rearrange("p (b d) -> p b d", b=3)
                ch(nc.vector.tensor_scalar_mul(y, o[:, 0, :], rc[:, s, 0:1]))
                ch(nc.vector.scalar_tensor_tensor(out=y, in0=o[:, 1, :], scalar=rc[:, s, 1:2], in1=y,
                                                  op0=ALU.mult, op1=ALU.add))
                last = nc.vector.scalar_tensor_tensor(out=y, in0=o[:, 2, :], scalar=rc[:, s, 2:3], in1=y,
                                                      op0=ALU.mult, op1=ALU.add)
                last.then_inc(merged, 1)

            with dve.Fori(0, G) as hh:
                ch.enter(hh, 5 * U)
                dve.wait_ge(rb_r, hh + 1)
                score(hh, 0)
                for u in range(U):
                    if u + 1 < U:
                        score(hh, u + 1)
                    merge(hh, u)
            ch.leave(G)

        @block.tensor
        def _(pe):
            pe.sem_inc(pv, 2)

            def score(hh, u):
                qt, kvh, j0, ls, lw = shape(u)
                r = slice(kvh * HD, (kvh + 1) * HD)
                pe.wait_ge(sread, hh * U + (u + 1))
                lhsT = q_s[r, qt * P:(qt + 1) * P]
                for c in range(0, ls, 512):
                    n = min(512, ls - c)
                    nc.tensor.matmul(PSf[:, c:c + n], lhsT, M.Z[r, Z_KV + 2, c:c + n], start=True, stop=True)
                for c in range(0, lw, 512):
                    n = min(512, lw - c)
                    nc.tensor.matmul(PSf[:, WIN0 + c:WIN0 + c + n], lhsT,
                                     M.Z[r, Z_KV + 4, j0 * P + c:j0 * P + c + n], start=True, stop=True)
                nc.tensor.matmul(PSf[:, CMP0:CMP0 + NCP], lhsT, M.kcT[r, :], start=True, stop=True)\
                  .then_inc(scores, 1)

            def values(hh, u):
                qt, kvh, j0, ls, lw = shape(u)
                s = u % 2
                pe.wait_ge(probs, hh * U + (u + 1))
                for g, grp in enumerate(groups(u)):
                    if first[u] + g >= 2:
                        pe.wait_ge(ptm, hh * NG + (first[u] + g - 1))
                    for n, (c, w) in enumerate(grp):
                        last = nc.tensor.transpose(M.PS[0:w, 4 + (first[u] + g) % 2, n * P:(n + 1) * P],
                                                   sbuf[:, s, c:c + w], M.ident[:, :])
                    last.then_inc(turned, 1)
                if u % 2 == 0 and u >= 2:
                    y_turn(hh, u // 2 - 1)
                pe.wait_ge(ptm, hh * NG + first[u + 1])
                pe.wait_ge(merged, hh * U + (u + 1))
                if u == 1:
                    pe.wait_ge(ym, hh * QT + 1)
                elif u % 2 == 1:
                    pe.wait_ge(ym, hh * QT + (u // 2 + 1))
                bank = M.PS[:, 6 + kvh, :]
                d = slice(kvh * HD, (kvh + 1) * HD)
                nw, ns = lw // P, ls // P
                at = [c for c, _ in tiles(u)]

                def p_of(c):
                    return pt[:, s, at.index(c) * P:(at.index(c) + 1) * P]

                nc.tensor.matmul(bank[:, 0:HD], p_of(CMP0)[0:NCP, :], M.vcp[0:NCP, d], start=True, stop=True)
                for n in range(ns):
                    nc.tensor.matmul(bank[:, HD:2 * HD], p_of(SEL0 + n * P),
                                     M.vtok[:, n, 0, d], start=(n == 0), stop=(n == ns - 1))
                for n in range(nw):
                    last = nc.tensor.matmul(bank[:, 2 * HD:3 * HD], p_of(WIN0 + n * P),
                                            M.vtok[:, j0 + n, 1, d], start=(n == 0), stop=(n == nw - 1))
                last.then_inc(pv, 1)

            def y_turn(hh, qt):
                pe.wait_ge(merged, hh * U + (2 * qt + 4))
                nc.tensor.transpose(M.PS[:, 7, 256:384], ytok[:, qt % 2, :], M.ident[:, :]).then_inc(yt, 1)

            pe.sem_inc(ym, 1)
            with pe.Fori(0, G) as hh:
                pe.wait_ge(q_r, hh + 1)
                score(hh, 0)
                for u in range(U):
                    if u + 1 < U:
                        score(hh, u + 1)
                    values(hh, u)
                y_turn(hh, QT - 1)


def phase_sample_setup(nc, M, A, O):
    M.bias = M.ring[0:H, :].rearrange("h (q m) -> h q m", q=2)
    small = M.misc[:, 2200:2560]
    M.pages = M.wg[0:1, :].bitcast(INT32)
    M.sl8, M.gsum, M.qb, M.newk = small[0:H, 0:1], small[0:H, 1:9], small[:, 9:17], small[:, 17:19]
    bs, sl, gs, bz = M.sem("bias_steps"), M.sem("slope_col"), M.sem("gsum_steps"), M.sem("qb_zeroed")
    with nc.Block() as block:
        @block.sync
        def _(sp):
            sp.dma_start(M.sl8, M.slope[0:1, :, :].rearrange("p k (g x) -> p (k g) x", x=1)).then_inc(sl, 16)
            sp.dma_start(M.pages, A["page_table"].rearrange("b n -> (b n)").rearrange("(a n) -> a n", a=1))\
              .then_inc(sl, 16)
            sp.wait_ge(sl, 32)

        @block.gpsimd
        def _(pool):
            pool.iota(M.bias, pattern=[[1, 2], [2, PAST // 2]], base=-PAST, channel_multiplier=0,
                      allow_small_or_imprecise_dtypes=True).then_inc(bs, 1)
            pool.memset(M.gsum, 1.0).then_inc(gs, 1)
            g2 = M.gsum.rearrange("p (g x) -> p g x", g=KVH)
            pool.wait_ge(gs, 1)
            pool.affine_select(out=g2, in_=g2, compare_op=ALU.is_ge, fill=0.0, base=0,
                               pattern=[[-G, KVH], [0, G]], channel_multiplier=1).then_inc(gs, 1)
            pool.wait_ge(gs, 2)
            pool.affine_select(out=g2, in_=g2, compare_op=ALU.is_ge, fill=0.0, base=G - 1,
                               pattern=[[G, KVH], [0, G]], channel_multiplier=-1).then_inc(gs, 1)
            pool.memset(M.qb, 0.0).then_inc(bz, 1)

        @block.vector
        def _(dve):
            dve.wait_ge(bs, 1)
            dve.wait_ge(sl, 32)
            nc.vector.tensor_scalar(M.bias, M.bias, M.sl8, None, ALU.mult)
            nc.vector.memset(M.misc[0:H, 1126 + NCS:1126 + 256], 0.0)


def phase_sample(nc, M, A, O):
    NT = NPAGES // 2
    HALF = PAST // 2
    Zf = M.Zf
    ringK = Zf[:, 4096:6144].rearrange("p (s c x) -> p s c x", s=4, c=4)
    ringV = Zf[:, 6144:6656].rearrange("p (s q x) -> p s q x", s=2, q=2)
    stage = Zf[:, 6656:7168].rearrange("p (s h q d) -> p s h q d", s=2, h=2, q=2)
    vslc = Zf[:, 7168:11264].rearrange("p (i q x) -> p i q x", i=NT, q=2)
    x2k = Zf[:, 11264:15360].rearrange("p (h r n) -> p h r n", h=2, r=8)
    x2v = Zf[:, 15360:19456].rearrange("p (h r n) -> p h r n", h=2, r=8)
    kslT = Zf[:, 19456:23552].rearrange("p (q m) -> p q m", q=2)
    wraw = Zf[:, 23552:24576].rearrange("p (c x) -> p c x", c=4)
    s = M.srow[0:H, 0:PAST + 1]
    sq = s[:, 0:PAST].rearrange("h (q m) -> h q m", q=2)
    hid = M.misc[:, 616:616 + 2 * NCS].rearrange("p (h n) -> p h n", h=2)
    kcT, pc = M.misc[:, 1126:1126 + NCS], M.misc[0:H, 1126:1126 + 256]
    kwT, sw = M.misc[:, 1382:1382 + WIN], M.misc[0:H, 1382:1382 + WIN + 1]
    pT = M.misc[:, 1896:1896 + 304]
    vc = [M.misc[:, 0:P], M.misc[:, 2240:2240 + P]]
    vn = [Zf[0:1, 24576:24704], M.misc[0:1, 2368:2368 + P]]
    sc = M.misc[0:H, 2496:2560]
    top = sc[:, 0:8]
    spare = M.gt[0:H, :, :].rearrange("p t g -> p (t g)")
    imp, pen = spare[:, 0:NSELS], spare[:, NSELS:2 * NSELS]
    neg, sm, mx, rcp = sc[:, 8:12], sc[:, 12:16], sc[:, 16:20], sc[:, 20:24]
    y8 = M.misc[0:H, 1382:1382 + P]
    S = M.sem
    kl = [S(f"k_tile{i}_loaded") for i in range(4)]
    vl = [S(f"v_tile{i}_loaded") for i in range(2)]
    kst, vst = S("k_tile_staged"), S("v_tile_staged")
    vsl, wl, vnl = S("vslc_loaded"), S("win_loaded"), S("vnew_loaded")
    ktd, kcm, ksm = S("k_tile_turned"), S("k_cmp_moved"), S("k_slc_moved")
    vtd, vcm = S("v_tile_turned"), S("v_cmp_moved")
    qbr, qkd, qkm, nwd, nwm = S("qb_ready"), S("qk_done"), S("qk_moved"), S("new_done"), S("new_moved")
    kwt, kwm, qwd, swm = S("kw_turned"), S("kw_moved"), S("qk_win_done"), S("win_max")
    cvd, gel, kcd, kcv = S("conv_done"), S("gelu_done"), S("kc_done"), S("kc_moved")
    qcd, cmx, exc, impr = S("qk_cmp_done"), S("cmp_max"), S("cmp_exp"), S("imp_ready")
    gsd, gsr, smx, exs, exw = S("imp_summed"), S("imp_read"), S("sel_max"), S("sel_exp"), S("win_exp")
    vcd, vcv, ptd, ptm = S("vc_done"), S("vc_moved"), S("sample_p_turned"), S("sample_p_moved")
    pvd, y8r, y8t, y8m, step = S("sample_pv"), S("y8_ready"), S("y8_turned"), S("y8_moved"), S("sample_step")
    pasv, pasp = S("sample_passed_dve"), S("sample_passed_pe")
    cache = A["cache_nsa_kv"][0].rearrange("g (m q) (w v) h d -> g m (q w) v (h d)", q=2, w=2)
    cache4 = A["cache_nsa_kv"][0].rearrange("g (m q) (w v) h d -> g m q w v (h d)", q=2, w=2)
    npool = A["cache_nsa_kv"].shape[1]

    with nc.Block() as block:
        @block.sync
        def _(sp):
            def page(b, i, half):
                return sp.value_load(M.pages[0:1, ds(b * NPAGES + (2 * i + half), 1)], min_val=0, max_val=npool - 1)

            def load_k(b):
                for i in range(NT):
                    sp.wait_ge(ktd, b * NT + (i + 1))
                    for half in range(2):
                        sp.dma_start(ringK[half * 64:half * 64 + 64, i % 4, :, :],
                                     cache[ds(page(b, i, half), 1), :, :, 0, :].rearrange("g m c x -> (g m) c x"))\
                          .then_inc(kl[i % 4], 16)

            def load_v(b):
                for i in range(NT):
                    sp.wait_ge(vst, b * NT + (i + 1))
                    for half in range(2):
                        sp.dma_start(ringV[half * 64:half * 64 + 64, i % 2, :, :],
                                     cache4[ds(page(b, i, half), 1), :, :, 0, 1, :].rearrange("g m q x -> (g m) q x"))\
                          .then_inc(vl[i % 2], 16)

            def load_rest(b):
                sp.wait_ge(pvd, b + 1)
                sp.dma_start(wraw, A["state_nsa_win"][0, ds(b, 1)].rearrange("b (c p) w h d -> p (b c) (w h d)", p=P))\
                  .then_inc(wl, 16)
                sp.dma_start(vn[0], O["kv_sample"][0, ds(b, 1), 0, 3].rearrange("b h d -> b (h d)")).then_inc(vnl, 16)
                sp.dma_start(vn[1], O["win_sample"][0, ds(b, 1), WIN - 1, 1].rearrange("b h d -> b (h d)"))\
                  .then_inc(vnl, 16)

            def load_vslc(b):
                for i in range(NT):
                    for half in range(2):
                        sp.dma_start(vslc[half * 64:half * 64 + 64, i, :, :],
                                     cache4[ds(page(b, i, half), 1), :, :, 1, 1, :].rearrange("g m q x -> (g m) q x"))\
                          .then_inc(vsl, 16)

            load_k(0)
            with sp.Fori(0, B - 1) as b:
                load_rest(b)
                load_v(b)
                load_vslc(b)
                load_k(b + 1)
            load_rest(B - 1)
            load_v(B - 1)
            load_vslc(B - 1)

        @block.gpsimd
        def _(pool):
            def put(src, i, sem):
                out = stage[:, i % 2].rearrange("p h q d -> p q h d")
                src = src.rearrange("p q (h d) -> p q h d", h=2)
                one = M.one[:, :].rearrange("p (q h d) -> p q h d", q=1, h=1).to_broadcast([P, 2, 2, HD])
                pool.tensor_tensor(out, src, one, ALU.mult).then_inc(sem, 1)

            def stage_k(b, i, head=False):
                pool.wait_ge(kl[i % 4], b * 128 + 32 * (i // 4 + 1))
                if i >= 2:
                    pool.wait_ge(ktd, b * NT + (i + 3))
                elif not head:
                    pool.wait_ge(vtd, b * NT + (i - 1))
                put(ringK[:, i % 4, 0:4:2, :], i, kst)

            def stage_v(b, i):
                pool.wait_ge(vl[i % 2], b * 256 + 32 * (i // 2 + 1))
                if i >= 2:
                    pool.wait_ge(vtd, b * NT + (i - 1))
                else:
                    pool.wait_ge(ktd, b * NT + (NT + i + 3))
                put(ringV[:, i % 2, :, :], i, vst)

            pool.sem_inc(vst, 2)
            for i in range(NT):
                stage_k(0, i, head=True)
            with pool.Fori(0, B - 1) as b:
                for i in range(NT):
                    stage_v(b, i)
                for i in range(NT):
                    stage_k(b + 1, i)
            for i in range(NT):
                stage_v(B - 1, i)

        @block.tensor
        def _(pe):
            pe.sem_inc(ktd, 4)
            pe.sem_inc(pvd, 1)

            def turn_k(b, i, head=False):
                pe.wait_ge(kst, b * NT + (i + 1))
                if i >= 2:
                    pe.wait_ge(kcm, b * NT + (i - 1))
                    pe.wait_ge(ksm, b * NT + (i - 1))
                elif not head:
                    pe.wait_ge(vcm, b * NT + (i - 1))
                    pe.wait_ge(qkm, b * 8)
                for q in range(2):
                    nc.tensor.transpose(M.PS[:, 3 + i % 2, q * P:(q + 1) * P], ringK[:, i % 4, 2 * q + 1, :],
                                        M.ident[:, :])
                for h in range(2):
                    last = nc.tensor.transpose(M.PS[:, 1 + i % 2, h * P:(h + 1) * P],
                                               stage[:, i % 2, h].rearrange("p q d -> p (q d)"), M.ident[:, :])
                last.then_inc(ktd, 1)

            def turn_v(b, i):
                pe.wait_ge(vst, b * NT + (i + 3))
                if i >= 2:
                    pe.wait_ge(vcm, b * NT + (i - 1))
                else:
                    pe.wait_ge(kcm, b * NT + (NT - 1 + i))
                for h in range(2):
                    last = nc.tensor.transpose(M.PS[:, 1 + i % 2, h * P:(h + 1) * P],
                                               stage[:, i % 2, h].rearrange("p q d -> p (q d)"), M.ident[:, :])
                last.then_inc(vtd, 1)

            def conv(v, bank, x2, j):
                return nc.tensor.matmul(M.PS[:, bank, 0:2 * NCS], M.w1[:, v, j, :],
                                        x2[:, :, j % 8, j // 8:j // 8 + NCS], start=(j == 0), stop=(j == 15))

            def body(b, more):
                pe.wait_ge(qbr, b + 1)
                pe.wait_ge(ksm, b * NT + NT)
                for c in range(8):
                    if c >= 2:
                        pe.wait_ge(qkm, b * 8 + (c - 1))
                    nc.tensor.matmul(M.PS[0:H, 3 + c % 2, :], M.qb, kslT[:, c // 4, (c % 4) * 512:(c % 4 + 1) * 512],
                                     start=True, stop=True).then_inc(qkd, 1)
                pe.wait_ge(y8m, b + 1)
                for n in range(2):
                    last = nc.tensor.matmul(M.PS[0:H, 5, 400 + n:401 + n], M.qb, M.newk[:, n:n + 1],
                                            start=True, stop=True)
                last.then_inc(nwd, 1)
                pe.wait_ge(wl, b * 16 + 16)
                for c in range(4):
                    last = nc.tensor.transpose(M.PS[:, 6, c * P:(c + 1) * P], wraw[:, c, 0:P], M.ident[:, :])
                last.then_inc(kwt, 1)
                for i in range(NT):
                    turn_v(b, i)
                    if i == 0:
                        pe.wait_ge(kcm, b * NT + NT)
                    last = conv(0, 0, x2k, i)
                    if i == 8:
                        pe.wait_ge(kwm, b + 1)
                        pe.wait_ge(y8r, b + 1)
                        nc.tensor.matmul(M.PS[0:H, 7, :], M.qb, kwT, start=True, stop=True).then_inc(qwd, 1)
                last.then_inc(cvd, 1)
                for i in range(NT):
                    if more:
                        turn_k(b + 1, i)
                    if i == 0:
                        pe.wait_ge(vcm, b * NT + NT)
                    last = conv(1, 6, x2v, i)
                    if i == 2:
                        pe.wait_ge(gel, 2 * b + 1)
                        pe.wait_ge(nwm, b + 1)
                        for h in range(2):
                            kc = nc.tensor.matmul(M.PS[h * HD:(h + 1) * HD, 5, 0:NCS], M.w2[:, 0, :], hid[:, h, :],
                                                  start=True, stop=True)
                        kc.then_inc(kcd, 1)
                    if i == 5:
                        pe.wait_ge(kcv, b + 1)
                        pe.wait_ge(swm, b + 1)
                        nc.tensor.matmul(M.PS[0:H, 7, 0:NCS], M.qb, kcT, start=True, stop=True).then_inc(qcd, 1)
                    if i == 10:
                        pe.wait_ge(impr, b + 1)
                        pe.sem_inc(pasp, 1)
                        nc.tensor.matmul(M.PS[0:H, 5, 0:64], M.gsum, imp[:, 0:64], start=True, stop=True)\
                          .then_inc(gsd, 1)
                last.then_inc(cvd, 1)
                pe.wait_ge(gel, 2 * b + 2)
                pe.wait_ge(gsr, b + 1)
                for n in range(2):
                    w = min(P, NCS - n * P)
                    for h in range(2):
                        last = nc.tensor.matmul(M.PS[0:w, 5, n * P + h * HD:n * P + (h + 1) * HD],
                                                hid[:, h, n * P:n * P + w], M.w2[:, 1, :], start=True, stop=True)
                last.then_inc(vcd, 1)
                id8 = M.ident[0:H, 0:H]
                pe.wait_ge(exw, b + 1)
                pe.sem_inc(pasp, 1)
                for c in range(4):
                    nc.tensor.transpose(M.PS[:, 6, 256 + c * H:256 + (c + 1) * H], sw[:, c * P:(c + 1) * P], id8)
                for n in range(2):
                    w = min(P, NCS - n * P)
                    nc.tensor.transpose(M.PS[0:w, 6, 288 + n * H:288 + (n + 1) * H], pc[:, n * P:n * P + w], id8)
                pe.wait_ge(exs, b + 1)
                pe.sem_inc(pasp, 1)
                for c in range(2 * NT):
                    nc.tensor.transpose(M.PS[:, 6, c * H:(c + 1) * H], s[:, c * P:(c + 1) * P], id8)
                nc.tensor.transpose(M.PS[0:1, 6, 304:304 + H], s[:, PAST:PAST + 1], id8)
                nc.tensor.transpose(M.PS[0:1, 6, 312:312 + H], sw[:, WIN:WIN + 1], id8).then_inc(ptd, 1)
                pe.wait_ge(ptm, b + 1)
                pe.wait_ge(vsl, b * 512 + 512)
                pe.wait_ge(vnl, b * 32 + 32)
                pe.wait_ge(vcv, b + 1)
                o = M.PS[0:H, 7, :]
                for c in range(2 * NT):
                    nc.tensor.matmul(o[:, P:2 * P], pT[:, c * H:(c + 1) * H], vslc[:, c % NT, c // NT, :],
                                     start=(c == 0), stop=False)
                nc.tensor.matmul(o[:, P:2 * P], M.pn[:, 0:H], vn[0], start=False, stop=True)
                for c in range(4):
                    nc.tensor.matmul(o[:, 2 * P:3 * P], pT[:, 256 + c * H:256 + (c + 1) * H], wraw[:, c, P:2 * P],
                                     start=(c == 0), stop=False)
                nc.tensor.matmul(o[:, 2 * P:3 * P], M.pn[:, H:2 * H], vn[1], start=False, stop=True)
                for n in range(2):
                    w = min(P, NCS - n * P)
                    last = nc.tensor.matmul(o[:, 0:P], pT[0:w, 288 + n * H:288 + (n + 1) * H], vc[n][0:w, :],
                                            start=(n == 0), stop=(n == 1))
                last.then_inc(pvd, 1)
                pe.wait_ge(y8r, b + 2)
                pe.sem_inc(pasp, 1)
                nc.tensor.transpose(M.PS[:, 5, 256:256 + H], y8, id8).then_inc(y8t, 1)

            for i in range(NT):
                turn_k(0, i, head=True)
            with pe.Fori(0, B - 1) as b:
                body(b, True)
            body(B - 1, False)

        @block.scalar
        def _(act):
            act.sem_inc(y8m, 1)

            def move(psb, x2, i, sem):
                nc.scalar.activation(x2[:, :, :, i * 16:(i + 1) * 16],
                                     M.PS[:, psb, 0:256].rearrange("p (h n r) -> p h r n", h=2, r=8),
                                     ACT.Copy).then_inc(sem, 1)

            def move_k(b, i):
                act.wait_ge(ktd, b * NT + (i + 5))
                move(1 + i % 2, x2k, i, kcm)

            def gelu(b, v):
                act.wait_ge(cvd, 2 * b + (v + 1))
                nc.scalar.activation(hid.rearrange("p h n -> p (h n)"), M.PS[:, (0, 6)[v], 0:2 * NCS],
                                     ACT.Gelu_apprx_tanh, bias=M.hb[:, v:v + 1]).then_inc(gel, 1)

            def body(b, more):
                act.wait_ge(kwt, b + 1)
                nc.scalar.activation(kwT, M.PS[:, 6, :], ACT.Copy).then_inc(kwm, 1)
                for i in range(NT):
                    act.wait_ge(vtd, b * NT + (i + 1))
                    move(1 + i % 2, x2v, i, vcm)
                gelu(b, 0)
                for i in range(NT):
                    if more:
                        move_k(b + 1, i)
                    if i == 3:
                        act.wait_ge(kcd, b + 1)
                        nc.scalar.activation(kcT, M.PS[:, 5, 0:NCS], ACT.Copy).then_inc(kcv, 1)
                    if i == 7:
                        act.wait_ge(swm, b + 1)
                        nc.scalar.activation(sw, sw, ACT.Exp, bias=neg[:, 2:3], accum_out=sm[:, 2:3]).then_inc(exw, 1)
                        act.wait_ge(cmx, b + 1)
                        nc.scalar.activation(pc[:, 0:NCS], pc[:, 0:NCS], ACT.Exp, bias=neg[:, 0:1],
                                             accum_out=sm[:, 0:1]).then_inc(exc, 1)
                gelu(b, 1)
                act.wait_ge(vcd, b + 1)
                for n in range(2):
                    w = min(P, NCS - n * P)
                    last = nc.scalar.activation(vc[n][0:w, :], M.PS[0:w, 5, n * P:(n + 1) * P], ACT.Copy)
                last.then_inc(vcv, 1)
                act.wait_ge(smx, b + 1)
                nc.scalar.activation(s, s, ACT.Exp, bias=neg[:, 1:2], accum_out=sm[:, 1:2]).then_inc(exs, 1)
                act.wait_ge(ptd, b + 1)
                w = NCS - P
                nc.scalar.activation(pT[:, 0:296], M.PS[:, 6, 0:296], ACT.Copy)
                nc.scalar.activation(pT[0:w, 296:304], M.PS[0:w, 6, 296:304], ACT.Copy)
                nc.scalar.activation(M.pn[:, :], M.PS[0:1, 6, 304:320], ACT.Copy).then_inc(ptm, 1)
                act.wait_ge(y8t, b + 1)
                for k in range(KVH):
                    r = slice(k * HD, (k + 1) * HD)
                    last = nc.scalar.activation(M.hT[r, 4:8, ds(T + b, 1)].rearrange("p a n -> p (a n)"),
                                                M.PS[r, 5, 256 + k * G:256 + (k + 1) * G], ACT.Copy)
                last.then_inc(y8m, 1)

            for i in range(NT):
                move_k(0, i)
            with act.Fori(0, B - 1) as b:
                body(b, True)
            body(B - 1, False)

        @block.vector
        def _(dve):
            ch = Chain(dve, step)
            dve.sem_inc(y8r, 1)

            def move_s(b, i):
                dve.wait_ge(ktd, b * NT + (i + 5))
                nc.vector.tensor_copy(kslT[:, :, i * P:(i + 1) * P],
                                      M.PS[:, 3 + i % 2, 0:256].rearrange("p (q m) -> p q m", q=2)).then_inc(ksm, 1)

            def body(b, more):
                for k in range(KVH):
                    r = slice(k * HD, (k + 1) * HD)
                    nc.vector.tensor_scalar(M.qb[r, k * G:(k + 1) * G].rearrange("p (a n) -> p a n", n=1),
                                            M.zs[r, Z_Q:Z_Q + 4, ds(b, 1)], HD ** -0.5, None, ALU.mult)
                nc.vector.tensor_copy(M.newk.rearrange("p (a n) -> p a n", n=1),
                                      M.zs[:, Z_KV + 2:Z_KV + 5:2, ds(b, 1)]).then_inc(qbr, 1)
                for c in range(8):
                    dve.wait_ge(qkd, b * 8 + (c + 1))
                    part = slice((c % 4) * 512, (c % 4 + 1) * 512)
                    nc.vector.tensor_tensor(sq[:, c // 4, part], M.PS[0:H, 3 + c % 2, :], M.bias[:, c // 4, part],
                                            ALU.add).then_inc(qkm, 1)
                dve.wait_ge(nwd, b + 1)
                nc.vector.tensor_copy(s[:, PAST:PAST + 1], M.PS[0:H, 5, 400:401])
                nc.vector.tensor_copy(mx[:, 2:3], M.PS[0:H, 5, 400:401])
                dve.wait_ge(qwd, b + 1)
                nc.vector.tensor_copy(sw[:, WIN:WIN + 1], M.PS[0:H, 5, 401:402]).then_inc(nwm, 1)
                ch(nc.vector.tensor_tensor(sw[:, 0:WIN].rearrange("h (m q) -> h m q", q=2),
                                           M.PS[0:H, 7, :].rearrange("h (m q) -> h m q", q=2),
                                           M.bias[:, :, HALF - WIN // 2:HALF].rearrange("h q m -> h m q"), ALU.add))
                ch(nc.vector.reduce_max(mx[:, 3:4], sw, AX.X))
                nc.vector.tensor_scalar_mul(neg[:, 2:3], mx[:, 3:4], -1.0).then_inc(swm, 1)
                for i in range(NT):
                    if more:
                        move_s(b + 1, i)
                    if i == 6:
                        dve.wait_ge(qcd, b + 1)
                        ch(nc.vector.tensor_tensor(pc[:, 0:NCS], M.PS[0:H, 7, 0:NCS],
                                                   M.bias[:, 1, CLEN // 2 - 1:HALF:CSTR // 2], ALU.add))
                        ch(nc.vector.reduce_max(mx[:, 0:1], pc[:, 0:NCS], AX.X))
                        nc.vector.tensor_scalar_mul(neg[:, 0:1], mx[:, 0:1], -1.0).then_inc(cmx, 1)
                    if i == 9:
                        dve.wait_ge(exc, b + 1)
                        ch(nc.vector.reciprocal(rcp[:, 0:1], sm[:, 0:1]))
                        ch(nc.vector.tensor_scalar(pc[:, 0:NCS], pc[:, 0:NCS], rcp[:, 0:1], None, ALU.mult))
                        ch(nc.vector.reduce_sum(imp[:, 0:64], pc.rearrange("h (s n) -> h s n", n=4), AX.X))
                        nc.vector.tensor_tensor(imp[:, 1:64], imp[:, 1:64], pc[:, 3:252:4], ALU.add)\
                          .then_inc(impr, 1)
                    if i == 12:
                        dve.wait_ge(gsd, b + 1)
                        ch(nc.vector.tensor_copy(imp[:, 0:64], M.PS[0:H, 5, 0:64]))
                        nc.vector.memset(imp[:, 0:1], 1e9).then_inc(gsr, 1)
                        ch(nc.vector.memset(imp[:, 63:65], 1e9))
                        for n in range(TOPK // 8):
                            dve.sem_inc(pasv, 1)
                            ch(nc.vector.max(top, imp))
                            dve.sem_inc(pasv, 1)
                            ch(nc.vector.match_replace(imp, top, imp, -2e9))
                        ch(nc.vector.tensor_scalar(pen, imp, -1.5e9, MASKED, ALU.is_gt, ALU.mult))
                        dve.sem_inc(pasv, 1)
                        for q in range(2):
                            last = nc.vector.tensor_tensor_reduce(
                                out=sq[:, q, :].rearrange("h (s m) -> h s m", m=SELB // 2),
                                in0=sq[:, q, :].rearrange("h (s m) -> h s m", m=SELB // 2),
                                in1=pen[:, 0:64].rearrange("h (s m) -> h s m", m=1).to_broadcast([H, 64, SELB // 2]),
                                scale=1.0, scalar=FLOOR, op0=ALU.add, op1=ALU.max, accum_out=mx[:, q:q + 1])
                        ch(last)
                        ch(nc.vector.reduce_max(rcp[:, 1:2], mx[:, 0:3], AX.X))
                        nc.vector.tensor_scalar_mul(neg[:, 1:2], rcp[:, 1:2], -1.0).then_inc(smx, 1)
                dve.wait_ge(exs, b + 1)
                ch(nc.vector.reciprocal(rcp[:, 1:3], sm[:, 1:3]))
                gates = M.sg[:, :, ds(b, 1)]
                r3 = rcp[:, 1:3].rearrange("h (b x) -> h b x", x=1)
                ch(nc.vector.tensor_tensor(r3, r3, gates[:, 1:3, :], ALU.mult))
                nc.vector.tensor_copy(rcp[:, 0:1].rearrange("h (b x) -> h b x", x=1), gates[:, 0:1, :])
                o = M.PS[0:H, 7, :]
                dve.wait_ge(pvd, b + 2)
                ch(nc.vector.tensor_scalar_mul(y8, o[:, P:2 * P], rcp[:, 1:2]))
                ch(nc.vector.scalar_tensor_tensor(out=y8, in0=o[:, 2 * P:3 * P], scalar=rcp[:, 2:3], in1=y8,
                                                  op0=ALU.mult, op1=ALU.add))
                nc.vector.scalar_tensor_tensor(out=y8, in0=o[:, 0:P], scalar=rcp[:, 0:1], in1=y8,
                                               op0=ALU.mult, op1=ALU.add).then_inc(y8r, 1)

            for i in range(NT):
                move_s(0, i)
            with dve.Fori(0, B - 1) as b:
                ch.enter(b, SAMPLE_STEPS)
                body(b, True)
            ch.leave(B - 1)
            body(B - 1, False)


def phase_mix_out(nc, M, A):
    ready = [M.sem(f"weights{s}_ready") for s in range(2)]
    done, moved = M.sem("tile_done"), M.sem("tile_moved")
    gla = A["w_out"][0, 0:GH * DV].rearrange("(k p) c -> p k c", p=P)
    nsa = A["w_out"][0, GH * DV:].rearrange("(q g d) c -> q d g c", q=KVH, d=HD)

    def rhs(k, c):
        return M.hT[:, k, c * CH:(c + 1) * CH]

    def load(sp, s, c):
        sp.dma_start(M.wt[:, s, 0:4, :], gla[:, :, c]).then_inc(ready[s], 16)
        for q in range(KVH):
            sp.dma_start(M.wt[q * HD:(q + 1) * HD, s, 4:8, :], nsa[q, :, :, c]).then_inc(ready[s], 16)

    with nc.Block() as block:
        @block.sync
        def _(sp):
            for s in range(2):
                load(sp, s, slice(s * P, (s + 1) * P))
            with sp.Fori(1, KD // 2) as i:
                for s in range(2):
                    sp.wait_ge(done, 2 * i + (s - 1))
                    load(sp, s, ds(i * 256 + s * P, P))

        @block.tensor
        def _(pe):
            for s in range(2):
                pe.wait_ge(ready[s], 48)
                dense_tile(nc, M, pe, s, KD, rhs, done)
            with pe.Fori(1, KD // 2) as i:
                for s in range(2):
                    pe.wait_ge(ready[s], 48 * i + 48)
                    pe.wait_ge(moved, 2 * i + (s - 1))
                    dense_tile(nc, M, pe, s, KD, rhs, done)

        @block.scalar
        def _(act):
            with act.Fori(0, KD // 2) as i:
                for s in range(2):
                    act.wait_ge(done, 2 * i + (s + 1))
                    nc.scalar.activation(M.Z[:, ds(2 * i + (16 + s), 1), :].rearrange("p a (c n) -> p (a c) n", n=CH),
                                         M.PS[:, 3 * s:3 * s + 3, 0:CH], ACT.Copy).then_inc(moved, 1)


def phase_ffn(nc, M, A):
    ready = [M.sem(f"weights{s}_ready") for s in range(2)]
    done, moved = M.sem("tile_done"), M.sem("tile_moved")
    up = A["w_ff_up"][0].rearrange("(k p) c -> p k c", p=P)
    KH = DFF // 2 // P
    down = A["w_ff_down"][0].rearrange("(f k p) c -> f p k c", f=2, p=P)
    relu = M.sem("ffn_relu")

    def banks(s):
        return M.PS[:, 3 * s:3 * s + 3, 0:CH]

    def z_tile(n):
        return M.Z[:, ds(n, 1), :].rearrange("p a (c n) -> p (a c) n", n=CH)

    segments = [(0, False, KD, KH), (0, True, KD + KH, KD), (1, False, 2 * KD + KH, KH),
                (1, True, 2 * (KD + KH), KD)]
    ready0 = (48 - 16) * KD // 2

    with nc.Block() as block:
        @block.sync
        def _(sp):
            for f, is_down, g, n in segments:
                with sp.Fori(0, n // 2) as i:
                    for s in range(2):
                        sp.wait_ge(done, 2 * i + (g + s + 1))
                        if is_down:
                            sp.dma_start(M.wt[:, s, 0:KH, :], down[f, :, :, ds(i * 256 + s * P, P)])\
                              .then_inc(ready[s], 16)
                        else:
                            sp.dma_start(M.wt[:, s, 0:KD, :], up[:, :, ds(i * 256 + (f * KH + s) * P, P)])\
                              .then_inc(ready[s], 16)

        @block.tensor
        def _(pe):
            pe.sem_inc(done, 2)
            for f, is_down, g, n in segments:
                src = M.Z if is_down else M.hT
                if is_down:
                    pe.wait_ge(moved, g + 2)
                with pe.Fori(0, n // 2) as i:
                    for s in range(2):
                        pe.wait_ge(ready[s], 16 * i + (16 * (g // 2 + 1) + ready0))
                        pe.wait_ge(moved, 2 * i + (g + s + 1))
                        dense_tile(nc, M, pe, s, KH if is_down else KD,
                                   lambda k, c: src[:, k, c * CH:(c + 1) * CH], done)

        @block.scalar
        def _(act):
            for f, is_down, g, n in segments:
                if not is_down:
                    with act.Fori(0, n // 2) as i:
                        for s in range(2):
                            act.wait_ge(done, 2 * i + (g + s + 3))
                            nc.scalar.activation(z_tile(2 * i + s), banks(s), ACT.Relu).then_inc(relu, 1)

        @block.vector
        def _(dve):
            dve.sem_inc(moved, 2)
            for f, is_down, g, n in segments:
                with dve.Fori(0, n // 2) as i:
                    for s in range(2):
                        if is_down:
                            dve.wait_ge(done, 2 * i + (g + s + 3))
                        else:
                            dve.wait_ge(relu, 2 * i + (f * KH + s + 1))
                        bank, out = banks(s), z_tile(2 * i + (16 * is_down + s))
                        if not is_down:
                            last = nc.vector.tensor_tensor(out, out, out, ALU.mult)
                        elif f == 0:
                            last = nc.vector.tensor_copy(out, bank)
                        else:
                            last = nc.vector.tensor_tensor(out, bank, out, ALU.add)
                        last.then_inc(moved, 1)


def phase_store(nc, M, O):
    st = M.ring[:, 0:2 * D].rearrange("p (s d) -> p s d", s=2)
    turned, stored = M.sem("y_tile_turned"), [M.sem(f"y_stored{s}") for s in range(2)]
    moved = [M.sem("y_by_act"), M.sem("y_by_dve")]
    yp = O["y_prompt"].rearrange("b (t p) d -> (b t) p d", p=P)
    with nc.Block() as block:
        @block.tensor
        def _(pe):
            for t in range(QT + 1):
                s, n = t % 2, (P if t < QT else B)
                if t >= 2:
                    for half in range(2):
                        pe.wait_ge(moved[half], t - 1)
                for k in range(KD):
                    last = nc.tensor.transpose(M.PS[0:n, 2 * s + k // 4, (k % 4) * P:(k % 4 + 1) * P],
                                               M.xT[:, k, t * P:t * P + n], M.ident[:, :])
                last.then_inc(turned, 1)

        def move(eng, copy, half):
            for t in range(QT + 1):
                s, n = t % 2, (P if t < QT else B)
                if t >= 2:
                    eng.wait_ge(stored[s], 16 * (t // 2))
                eng.wait_ge(turned, t + 1)
                copy(st[0:n, s, half * 512:(half + 1) * 512], M.PS[0:n, 2 * s + half, :]).then_inc(moved[half], 1)

        @block.scalar
        def _(act):
            move(act, lambda out, src: nc.scalar.activation(out, src, ACT.Copy), 0)

        @block.vector
        def _(dve):
            move(dve, nc.vector.tensor_copy, 1)

        @block.sync
        def _(sp):
            for t in range(QT + 1):
                s = t % 2
                for half in range(2):
                    sp.wait_ge(moved[half], t + 1)
                out = yp[t] if t < QT else O["y_sample"].rearrange("b s d -> (b s) d")
                sp.dma_start(out, st[0:P if t < QT else B, s, :]).then_inc(stored[s], 16)
            sp.wait_ge(stored[0], 16 * 5)
            sp.wait_ge(stored[1], 16 * 4)


OUTS = [
    ("y_prompt", (1, T, D)),
    ("y_sample", (B, 1, D)),
    ("kv_prompt", (1, 1, T, 4, KVH, HD)),
    ("kv_sample", (1, B, 1, 4, KVH, HD)),
    ("win_prompt", (1, 1, WIN, 2, KVH, HD)),
    ("win_sample", (1, B, WIN, 2, KVH, HD)),
    ("gla_prompt", (1, 1, GH, DK, DV)),
    ("gla_sample", (1, B, GH, DK, DV)),
]


def build(nc, A, O):
    M = Mem()
    with ExitStack() as ctx:
        layout(nc, ctx, M)
        phase_load(nc, M, A, O)
        phase_norm(nc, M, 0, M.xT, M.nw[:, 0], False, M.hT)
        phase_project(nc, M, A)
        phase_kv_rows(nc, M, A, O)
        phase_gla(nc, M, A, O)
        phase_compress(nc, M, A)
        phase_attend(nc, M)
        phase_sample_setup(nc, M, A, O)
        phase_sample(nc, M, A, O)
        phase_mix_out(nc, M, A)
        phase_norm(nc, M, 1, M.Z[:, 16:24, :], M.nw[:, 1], True, M.hT)
        phase_norm(nc, M, 2, M.xT, M.nw[:, 2], False, M.hT)
        phase_ffn(nc, M, A)
        phase_norm(nc, M, 3, M.Z[:, 16:24, :], M.nw[:, 3], True, M.hT)
        phase_store(nc, M, O)


def kernel(**inputs):
    import numpy as np
    import concourse.bacc as bacc
    from concourse.bass_utils import run_bass_kernel_spmd

    nc = bacc.Bacc("TRN2", target_bir_lowering=False, num_devices=1)
    arrays, A, O = {}, {}, {}
    for name, x in inputs.items():
        x = np.ascontiguousarray(x)
        arrays[f"in_{name}"] = x
        A[name] = nc.dram_tensor(f"in_{name}", x.shape, mybir.dt.from_np(x.dtype), kind="ExternalInput").ap()
    for name, shape in OUTS:
        O[name] = nc.dram_tensor(f"out_{name}", shape, FP32, kind="ExternalOutput").ap()
    build(nc, A, O)
    r = run_bass_kernel_spmd(nc, [arrays], core_ids=[0])
    return tuple(r.results[0][f"out_{name}"] for name, _ in OUTS)
```

```python
from contextlib import ExitStack

import concourse.bass as bass
from concourse import mybir

FP32 = mybir.dt.float32
INT32 = mybir.dt.int32
ALU = mybir.AluOpType
ACT = mybir.ActivationFunctionType
AX = mybir.AxisListType
ds = bass.ds

D = 1024
T = 1024
B = 8
N = T + B
P = 128
KD = D // P
CH = N // 3
PAST = 4096
PAGE = 128
NPAGES = PAST // PAGE
WIN = 512
GH, DK, DV = 4, 64, 128
CHUNK = 64
H, KVH, HD = 8, 2, 64
G = H // KVH
CLEN, CSTR, CHID = 32, 16, 128
SELB = 64
TOPK = 16
DFF = 4096
EPS = 1e-6
MASKED = -1e30
FLOOR = -1e20
QT = T // P
C_GQ, C_GK, C_GV, C_GR = 0, 256, 512, 1024
C_GLR, C_NQ, C_KV, C_NG = 1536, 1552, 2064, 2832
RANK = 16
NGATE = 3 * H
Z_GQ, Z_GK, Z_GV, Z_GR, Z_Q, Z_KV, Z_SM = 0, 2, 4, 8, 12, 16, 22
NCP = (T - CLEN) // CSTR + 1
NCS = (PAST + 1 - CLEN) // CSTR + 1
NSELS = PAST // SELB + 1
RSEL, RWIN, RCMP = 1024, 640, 119

SAMPLE_STEPS = 21


class Chain:

    def __init__(self, eng, sem):
        self.eng, self.sem, self.base, self.k = eng, sem, 0, 0

    def enter(self, i, per):
        self.start, self.per = self.k, per
        self.base, self.k = i * per + self.k, 0

    def leave(self, rounds):
        assert self.k == self.per, (self.k, self.per)
        self.base, self.k = 0, self.start + rounds * self.per

    def mark(self, ins):
        ins.then_inc(self.sem, 1)
        self.k += 1
        return self.base + self.k

    def __call__(self, ins):
        self.eng.wait_ge(self.sem, self.mark(ins))


class Mem:
    pass


def layout(nc, ctx, M):
    def sb(name, shape, dt=FP32):
        return ctx.enter_context(nc.sbuf_tensor(name, shape, dt))

    M.X = sb("X", [P, QT, D])
    M.hT = sb("hT", [P, KD, N])
    M.Zf = sb("Z", [P, 24 * N])
    M.Z = M.Zf[:, :].rearrange("p (a n) -> p a n", n=N)
    M.ring = sb("ring", [P, 4096])
    M.wt = M.ring[:, :].rearrange("p (s k c) -> p s k c", s=2, c=P)
    M.srow = sb("srow", [P, 4104])
    M.misc = sb("misc", [P, 2560])
    M.Xs = M.misc[0:B, 0:D]
    M.rows = M.srow[:, 0:2 * D].rearrange("p (a d) -> p a d", a=2)
    M.norm_steps = 0
    M.ident = sb("ident", [P, P])
    M.ones = sb("ones", [P, P])
    M.nw = sb("nw", [P, 2, KD])
    M.eps = sb("eps", [P, 1])
    M.one = sb("one", [P, 1])
    M.gn = sb("gn", [P, 1])
    M.bg = sb("bg", [P, 2])
    M.wg = sb("wg", [RANK, 256])
    M.gt = sb("gt", [P, QT, NGATE])
    M.sg = sb("sg", [B, 3, B])
    M.zs = sb("zs", [P, 22, B])
    M.pn = sb("pn", [1, 2 * H])
    M.PS = ctx.enter_context(nc.psum_tensor("PS", [P, 8, 512], FP32))
    M.sems = {}

    def sem(name):
        if name not in M.sems:
            M.sems[name] = ctx.enter_context(nc.semaphore(name))
        return M.sems[name]

    M.sem = sem


def phase_load(nc, M, A, O):
    gains, const = M.sem("gains_loaded"), M.sem("const_ready")
    M.NLOADS = 5

    with nc.Block() as block:
        @block.sync
        def _(sp):
            load_x(sp, M, A)

        @block.gpsimd
        def _(pool):
            c0 = M.sem("const_zeroed")
            pool.memset(M.ident[:, :], 0.0).then_inc(c0, 1)
            pool.wait_ge(c0, 1)
            pool.affine_select(out=M.ident[:, :], in_=M.ident[:, :], compare_op=ALU.not_equal, fill=1.0,
                               base=0, pattern=[[-1, P]], channel_multiplier=1).then_inc(const, 1)
            pool.memset(M.eps[:, :], EPS)
            pool.memset(M.one[:, :], 1.0)
            pool.memset(M.ones[:, :], 1.0).then_inc(const, 1)

        @block.scalar
        def _(act):
            for n, name in ((0, "norm_mix_pre"), (1, "norm_ffn_pre")):
                act.dma_start(M.nw[:, n, :], A[name].rearrange("a (k p) -> p (a k)", p=P),
                              allow_slow_non_contiguous=True).then_inc(gains, 16)
            act.dma_start(M.gn[:, :], A["gla_norm"].rearrange("a p -> p a"),
                          allow_slow_non_contiguous=True).then_inc(gains, 16)
            act.dma_start(M.bg[:, :], A["b_gla_gate"].rearrange("a (k p) -> p (a k)", p=P),
                              allow_slow_non_contiguous=True).then_inc(gains, 16)
            act.dma_start(M.wg[:, :], A["w_gla_gate"][0]).then_inc(gains, 16)
            act.wait_ge(gains, 16 * M.NLOADS)


def load_x(eng, M, A):
    xp = A["x_prompt"].rearrange("b (j t p) d -> (b j) p t d", t=2, p=P)
    for j in range(QT // 2):
        eng.dma_start(M.X[:, 2 * j:2 * j + 2, :], xp[j]).then_inc(M.sem(f"x_loaded{j}"), 16)
    eng.dma_start(M.Xs, A["x_sample"].rearrange("b s d -> (b s) d")).then_inc(M.sem("xs_loaded"), 16)


def x_tile(M, t):
    return M.X[:, t, :] if t < QT else M.Xs


def wait_x(eng, M, t, times):
    eng.wait_ge(M.sem(f"x_loaded{t // 2}" if t < QT else "xs_loaded"), 16 * times)


def phase_norms(nc, M, A, O, use, front, back):
    NT = QT + 1
    LAG, PLAG = (0, 0) if front is None else (2, 3)
    junk = M.Zf[:, 0:6 * D].rearrange("p (s d) -> p s d", s=6)
    tmp = M.Zf[:, 6 * D:8 * D].rearrange("p (s d) -> p s d", s=2)
    diag = M.Zf[:, 8 * D:8 * D + 2 * P].rearrange("p (s n) -> p s n", s=2)
    st = M.Zf[:, 9 * D:9 * D + 4 * NT].rearrange("p (a t) -> p a t", a=4)
    sf, f0 = ("front_turned", "front_squared", "front_scaled", "front_added"), (use - 1) * NT
    trn, sqa, stt, added = (M.sem(x) for x in sf)
    sqb, dgr, bkd, evd = (M.sem(x) for x in ("back_squared", "diag_ready", "back_turned", "hT_written"))
    rta, rtb = M.sem("front_root"), M.sem("back_root")
    b0 = use * NT
    step, stored = M.sem("norm_step"), M.sem("y_stored")
    out = O["y_prompt"].rearrange("b (t p) d -> (b t) p d", p=P)

    def toks(t):
        return P if t < QT else B

    with nc.Block() as block:
        @block.sync
        def _(sp):
            if use == 0:
                for s in range(2):
                    sp.dma_start(M.wt[:, s, 0:KD, :], A["w_in"][0, :, s * P:(s + 1) * P]
                                 .rearrange("(k p) c -> p k c", p=P)).then_inc(M.sem(f"win_ready{s}"), 16)
            elif back is not None:
                for s in range(2):
                    sp.dma_start(M.wt[:, s, 0:KD, :], A["w_ff_up"][0, :, s * P:(s + 1) * P]
                                 .rearrange("(k p) c -> p k c", p=P)).then_inc(M.sem(f"weights{s}_ready"), 16)
            else:
                for t in range(NT):
                    sp.wait_ge(added, f0 + t + 1)
                    dst = out[t] if t < QT else O["y_sample"].rearrange("b s d -> (b s) d")
                    sp.dma_start(dst, x_tile(M, t)).then_inc(stored, 16)
                sp.wait_ge(stored, 16 * NT)

        @block.tensor
        def _(pe):
            def turn_front(t):
                s, n = t % 2, toks(t)
                if t >= 2:
                    pe.wait_ge(stt, f0 + t - 1)
                for k in range(KD):
                    last = nc.tensor.transpose(M.PS[0:n, 2 * s + k // 4, (k % 4) * P:(k % 4 + 1) * P],
                                               M.Z[:, 16 + k, t * P:t * P + n], M.ident[:, :])
                last.then_inc(trn, 1)

            def turn_back(t):
                s, n = t % 2, toks(t)
                pe.wait_ge(dgr, b0 + t + 1)
                if t >= 2:
                    pe.wait_ge(evd, b0 + t - 1)
                for k in range(KD):
                    last = nc.tensor.matmul(M.PS[:, 4 + 2 * s + k // 4, (k % 4) * P:(k % 4) * P + n],
                                            x_tile(M, t)[:, k * P:(k + 1) * P], diag[0:n, s, 0:n],
                                            start=True, stop=True)
                last.then_inc(bkd, 1)

            for t in range(NT + PLAG):
                if front is not None and t < NT:
                    turn_front(t)
                if back is not None and t >= PLAG:
                    turn_back(t - PLAG)

        @block.scalar
        def _(act):
            for t in range(NT + LAG):
                if front is not None and t < NT:
                    n = toks(t)
                    act.wait_ge(trn, f0 + t + 1)
                    nc.scalar.activation(junk[0:n, t % 3, :].rearrange("p (b c) -> p b c", b=2),
                                         M.PS[0:n, 2 * (t % 2):2 * (t % 2) + 2, :],
                                         ACT.Square, accum_out=st[0:n, 0, t:t + 1]).then_inc(sqa, 1)
                    act.wait_ge(sqa, f0 + t + 1)
                    nc.scalar.activation(st[0:n, 1, t:t + 1], st[0:n, 0, t:t + 1], ACT.Sqrt, bias=M.eps[0:n, 0:1],
                                         scale=1.0 / D).then_inc(rta, 1)
                if back is not None and t >= LAG:
                    u = t - LAG
                    n = toks(u)
                    if front is None:
                        wait_x(act, M, u, 1)
                    else:
                        act.wait_ge(added, f0 + u + 1)
                    nc.scalar.activation(junk[0:n, 3 + u % 3, :], x_tile(M, u), ACT.Square,
                                         accum_out=st[0:n, 2, u:u + 1]).then_inc(sqb, 1)
                    act.wait_ge(sqb, b0 + u + 1)
                    nc.scalar.activation(st[0:n, 3, u:u + 1], st[0:n, 2, u:u + 1], ACT.Sqrt, bias=M.eps[0:n, 0:1],
                                         scale=1.0 / D).then_inc(rtb, 1)

        if front is not None:
            @block.gpsimd
            def _(pool):
                for t in range(NT):
                    n = toks(t)
                    pool.wait_ge(stt, f0 + t + 1)
                    if use == 1:
                        wait_x(pool, M, t, 2)
                    pool.tensor_tensor(x_tile(M, t), x_tile(M, t), tmp[0:n, t % 2, :], ALU.add).then_inc(added, 1)

        @block.vector
        def _(dve):
            ch = Chain(dve, step)
            ch.k = M.norm_steps

            def inverse(t, a):
                r = st[0:toks(t), a + 1, t:t + 1]
                ch(nc.vector.reciprocal(r, r))

            def scale_front(t):
                n = toks(t)
                dve.wait_ge(rta, f0 + t + 1)
                inverse(t, 0)
                if t == 0:
                    dve.wait_ge(M.sem("rows_loaded"), 32)
                if t >= 2:
                    dve.wait_ge(added, f0 + t - 1)
                nc.vector.scalar_tensor_tensor(out=tmp[0:n, t % 2, :].rearrange("p (b c) -> p b c", b=2),
                                               in0=M.PS[0:n, 2 * (t % 2):2 * (t % 2) + 2, :],
                                               scalar=st[0:n, 1, t:t + 1],
                                               in1=front[0:n, :].rearrange("p (b c) -> p b c", b=2),
                                               op0=ALU.mult, op1=ALU.mult).then_inc(stt, 1)

            def diagonal(t):
                n = toks(t)
                dve.wait_ge(rtb, b0 + t + 1)
                inverse(t, 2)
                if t >= 2:
                    dve.wait_ge(bkd, b0 + t - 1)
                nc.vector.tensor_scalar(diag[0:n, t % 2, 0:n], M.ident[0:n, 0:n], st[0:n, 3, t:t + 1], None,
                                        ALU.mult).then_inc(dgr, 1)

            def move(t):
                s, n = t % 2, toks(t)
                dve.wait_ge(bkd, b0 + t + 1)
                nc.vector.tensor_tensor(M.hT[:, :, t * P:t * P + n],
                                        M.PS[:, 4 + 2 * s:6 + 2 * s, :].rearrange("p b (k c) -> p (b k) c", c=P)[:, :, 0:n],
                                        back.rearrange("p (k x) -> p k x", x=1).to_broadcast([P, KD, n]),
                                        ALU.mult).then_inc(evd, 1)

            for t in range(NT + PLAG + 1):
                if front is not None and t < NT:
                    scale_front(t)
                if back is not None and LAG <= t < NT + LAG:
                    diagonal(t - LAG)
                if back is not None and t > PLAG:
                    move(t - PLAG - 1)
            M.norm_steps = ch.k


def dense_tile(nc, M, pe, s, kn, rhs, done):
    for k in range(kn):
        for c in range(3):
            last = nc.tensor.matmul(M.PS[:, 3 * s + c, 0:CH], M.wt[:, s, k, :], rhs(k, c),
                                    start=(k == 0), stop=(k == kn - 1))
    last.then_inc(done, 1)


def phase_project(nc, M, A):
    ready = [M.sem(f"win_ready{s}") for s in range(2)]
    done, moved = M.sem("proj_done"), M.sem("proj_moved")
    w = A["w_in"][0].rearrange("(k p) c -> p k c", p=P)

    def rhs(k, c):
        return M.hT[:, k, c * CH:(c + 1) * CH]

    def bank(s):
        return M.PS[:, 3 * s:3 * s + 3, 0:CH]

    with nc.Block() as block:
        @block.sync
        def _(sp):
            with sp.Fori(1, 6) as i:
                for s in range(2):
                    sp.wait_ge(done, 2 * i + (s - 1))
                    sp.dma_start(M.wt[:, s, 0:KD, :], w[:, :, ds(i * 256 + s * P, P)]).then_inc(ready[s], 16)
            for i in range(2):
                for s in range(2):
                    sp.wait_ge(done, 2 * (6 + i) + s - 1)
                    for half in range(2):
                        c = C_NQ + (2 * i + s + G * half) * HD
                        sp.dma_start(M.wt[:, s, 0:KD, half * HD:(half + 1) * HD], w[:, :, c:c + HD])\
                          .then_inc(ready[s], 16)
            with sp.Fori(0, 3) as i:
                for s in range(2):
                    sp.wait_ge(done, 2 * i + (16 + s - 1))
                    sp.dma_start(M.wt[:, s, 0:KD, :], w[:, :, ds(i * 256 + (C_KV + s * P), P)])\
                      .then_inc(ready[s], 16)
            sp.wait_ge(done, 21)
            sp.dma_start(M.wt[:, 0, 0:KD, 0:RANK], w[:, :, C_GLR:C_GLR + RANK]).then_inc(ready[0], 16)
            sp.dma_start(M.wt[:, 0, 0:KD, RANK:RANK + NGATE], w[:, :, C_NG:C_NG + NGATE]).then_inc(ready[0], 16)

        @block.tensor
        def _(pe):
            for s in range(2):
                pe.wait_ge(ready[s], 16)
                dense_tile(nc, M, pe, s, KD, rhs, done)
            with pe.Fori(1, 6) as i:
                for s in range(2):
                    pe.wait_ge(ready[s], 16 * i + 16)
                    pe.wait_ge(moved, 2 * i + (s - 1))
                    dense_tile(nc, M, pe, s, KD, rhs, done)
            for i in range(2):
                for s in range(2):
                    pe.wait_ge(ready[s], 16 * (6 + 2 * (i + 1)))
                    pe.wait_ge(moved, 2 * (6 + i) + s - 1)
                    dense_tile(nc, M, pe, s, KD, rhs, done)
            with pe.Fori(0, 3) as i:
                for s in range(2):
                    pe.wait_ge(ready[s], 16 * i + 16 * 11)
                    pe.wait_ge(moved, 2 * i + (16 + s - 1))
                    dense_tile(nc, M, pe, s, KD, rhs, done)
            pe.wait_ge(ready[0], 16 * 15)
            pe.wait_ge(moved, 21)
            for k in range(KD):
                for c in range(3):
                    last = nc.tensor.matmul(M.PS[0:RANK + NGATE, c, 0:CH], M.wt[:, 0, k, 0:RANK + NGATE], rhs(k, c),
                                            start=(k == 0), stop=(k == KD - 1))
            last.then_inc(done, 1)

        @block.scalar
        def _(act):
            with act.Fori(0, 11) as i:
                for s in range(2):
                    act.wait_ge(done, 2 * i + (s + 1))
                    nc.scalar.activation(M.Z[:, ds(2 * i + s, 1), :].rearrange("p a (c n) -> p (a c) n", n=CH),
                                         bank(s), ACT.Copy).then_inc(moved, 1)
            act.wait_ge(done, 23)
            nc.scalar.activation(M.Z[0:RANK + NGATE, Z_SM, :].rearrange("p (c n) -> p c n", n=CH),
                                 M.PS[0:RANK + NGATE, 0:3, 0:CH], ACT.Copy).then_inc(moved, 1)


def phase_kv_rows(nc, M, A, O):
    st = M.srow[:, 0:3 * 768].rearrange("p (s c) -> p s c", s=3)
    vtok = M.ring[:, 0:2048].rearrange("p (t b c) -> p t b c", t=QT, b=2)
    M.vtok = vtok
    turned, rows, vcop = M.sem("kv_turned"), M.sem("kv_rows"), M.sem("v_kept")
    expd, stored = M.sem("gate_exp"), [M.sem(f"rows_stored{s}") for s in range(3)]
    wmove, sgl, onep = M.sem("win_moved"), M.sem("sg_loaded"), M.sem("gate_onep")
    sgate = M.sem("sg_exp")
    kvp = O["kv_prompt"].rearrange("a b (t p) c k d -> (a b t) p (c k d)", p=P)
    wnp = O["win_prompt"].rearrange("a b (t p) c k d -> (a b t) p (c k d)", p=P)

    def stores_of_slot(t):
        return sum(1 + (u >= QT - WIN // P) for u in range(t % 2, t + 1, 2))

    with nc.Block() as block:
        @block.tensor
        def _(pe):
            for t in range(QT + 1):
                s, n = t % 2, (P if t < QT else B)
                if t >= 2:
                    pe.wait_ge(rows, t - 1)
                for j in range(6):
                    nc.tensor.transpose(M.PS[0:n, 2 * s + j // 4, (j % 4) * P:(j % 4 + 1) * P],
                                        M.Z[:, Z_KV + j, t * P:t * P + n], M.ident[:, :])\
                      .then_inc(turned, 1)
                if t < QT:
                    nc.tensor.transpose(M.PS[:, 2 * s + 1, 256:256 + 40], M.Z[0:40, Z_SM, t * P:t * P + n],
                                        M.ident[0:40, 0:40]).then_inc(turned, 1)

        @block.scalar
        def _(act):
            act.dma_start(O["win_sample"][0, :, 0:WIN - 1].rearrange("b r c k d -> b (r c k d)"),
                          A["state_nsa_win"][0, :, 1:WIN].rearrange("b r c k d -> b (r c k d)")).then_inc(wmove, 16)
            for br in range(3):
                act.dma_start(M.sg[:, br, :], M.Z[RANK + br * H:RANK + (br + 1) * H, Z_SM, T:N]).then_inc(sgl, 16)
            for t in range(QT + 1):
                s, n = t % 2, (P if t < QT else B)
                act.wait_ge(turned, 7 * t + (7 if t < QT else 6))
                if t >= 2:
                    act.wait_ge(stored[s], 16 * stores_of_slot(t - 2))
                    act.wait_ge(vcop, t - 1)
                if t < QT:
                    nc.scalar.activation(M.gt[:, t, :], M.PS[:, 2 * s + 1, 256 + RANK:256 + 40], ACT.Exp,
                                         scale=-1.0).then_inc(expd, 1)
                nc.scalar.activation(st[0:n, s, 0:512], M.PS[0:n, 2 * s, :], ACT.Copy)
                nc.scalar.activation(st[0:n, s, 512:768], M.PS[0:n, 2 * s + 1, 0:256], ACT.Copy)\
                  .then_inc(rows, 1)
            act.wait_ge(sgl, 48)
            nc.scalar.activation(M.sg[:, :, :], M.sg[:, :, :], ACT.Exp, scale=-1.0).then_inc(sgate, 1)
            act.wait_ge(wmove, 16)

        @block.gpsimd
        def _(pool):
            for t in range(QT):
                s = t % 2
                pool.wait_ge(rows, t + 1)
                pool.tensor_copy(vtok[:, t, 0, :], st[:, s, 384:512])
                pool.tensor_copy(vtok[:, t, 1, :], st[:, s, 640:768]).then_inc(vcop, 1)
            pool.tensor_copy(M.zs[:, :, :], M.Z[:, 0:22, T:N]).then_inc(vcop, 1)

        @block.vector
        def _(dve):
            dve.wait_ge(expd, QT)
            for buf, sem in ((M.gt, expd), (M.sg, sgate)):
                if buf is M.sg:
                    dve.wait_ge(sgate, 1)
                nc.vector.tensor_scalar_add(buf[:, :, :], buf[:, :, :], 1.0).then_inc(onep, 1)
                dve.wait_ge(onep, 1 if buf is M.gt else 2)
                nc.vector.reciprocal(buf[:, :, :], buf[:, :, :])

        @block.sync
        def _(sp):
            for t in range(QT):
                s = t % 2
                sp.wait_ge(rows, t + 1)
                sp.dma_start(kvp[t], st[:, s, 0:512]).then_inc(stored[s], 16)
                if t >= QT - WIN // P:
                    sp.dma_start(wnp[t - (QT - WIN // P)], st[:, s, 512:768]).then_inc(stored[s], 16)
            sp.wait_ge(rows, QT + 1)
            sp.dma_start(O["kv_sample"].rearrange("a b s c k d -> (a b s) (c k d)"), st[0:B, 0, 0:512])\
              .then_inc(stored[0], 16)
            sp.dma_start(O["win_sample"][0, :, WIN - 1].rearrange("b c k d -> b (c k d)"), st[0:B, 0, 512:768])\
              .then_inc(stored[0], 16)
            sp.wait_ge(stored[0], 16 * 8)
            sp.wait_ge(stored[1], 16 * 6)


def phase_gla(nc, M, A, O):
    gT = M.srow[:, 0:2 * N].rearrange("p (a n) -> p a n", a=2)
    soft = [M.Z[:, 23, :], M.srow[:, 2 * N:3 * N]]
    tri = M.ring[:, 2048:2048 + P]

    def pair(base, buf=M.misc, n=2):
        return buf[:, base:base + n * P].rearrange("p (a n) -> p a n", a=n)

    bt, eb, enb, dl = pair(0), pair(256), pair(512), pair(768)
    qe, ke, kl = pair(1024), pair(1280), pair(1536)
    Sa, Sb = pair(1792), pair(2048)
    eg = M.misc[:, 2304:2320].rearrange("p (b a) -> p b a", a=2)
    qs = M.misc[:, 2320:2336].rearrange("p (a b) -> p a b", a=2)
    v_s, vtk = pair(2064, M.srow, 4), pair(2576, M.srow, 4)
    kltk, Am = pair(3088, M.srow), pair(3344, M.srow, 4)
    Amq = Am.rearrange("p (q a) n -> p q a n", q=2)
    state = M.srow[:, 0:2 * B * DV].rearrange("p (b a v) -> p b a v", b=B, a=2)
    dg = pair(2064, M.srow, 4)
    X, Y, OB, DS, VT, KT = 0, 1, 2, 4, 6, 7
    EXP = ACT.Exp
    S = M.sem
    xg, absd, soft_r, g_ready = S("gate_x"), S("gate_abs"), S("gate_soft"), S("gate_ready")
    step = S("gla_dve_step")
    scan, dlr, ebr, edl = S("scan_ready"), S("dl_ready"), S("eb_ready"), S("edl_ready")
    qk, klr, vst, vtd, ktd = S("qk_ready"), S("kl_ready"), S("v_static"), S("v_turned"), S("kl_turned")
    vke, ar, amr, dsr, in0 = S("vk_rows"), S("a_ready"), S("am_ready"), S("ds_ready"), S("inter0")
    sbr, sar, orr, oev = S("sb_ready"), S("sa_ready"), S("o_ready"), S("o_moved")
    tri_r, st_l, egr, dgr, vb = S("tri_ready"), S("state_loaded"), S("eg_ready"), S("dg_ready"), S("vb_ready")
    stn, so, stored, soe, qsr = S("state_new"), S("so_ready"), S("gla_stored"), S("so_moved"), S("qs_ready")
    sq, ss, rt, den, rs, mixed = S("o_sq"), S("o_ss"), S("o_root"), S("o_exp"), S("o_scaled"), S("o_mixed")

    with nc.Block() as block:
        @block.gpsimd
        def _(pool):
            t0 = S("tri_steps")
            pool.memset(tri, 1.0).then_inc(t0, 1)
            pool.wait_ge(t0, 1)
            pool.affine_select(out=tri, in_=tri, compare_op=ALU.is_ge, fill=0.0, base=0,
                               pattern=[[1, P]], channel_multiplier=-1).then_inc(t0, 1)
            pool.wait_ge(t0, 2)
            pool.affine_select(out=tri[:, CHUNK:P], in_=tri[:, CHUNK:P], compare_op=ALU.is_ge, fill=0.0,
                               base=-CHUNK, pattern=[[0, CHUNK]], channel_multiplier=1).then_inc(tri_r, 1)
            pool.wait_ge(g_ready, 2)
            with pool.Fori(0, QT) as t:
                pool.wait_ge(vtd, t + 1)
                pool.tensor_copy(v_s, M.Z[:, Z_GV:Z_GV + 4, ds(t * P, P)]).then_inc(vst, 1)

        @block.scalar
        def _(act):
            for a in range(2):
                act.wait_ge(xg, a + 1)
                nc.scalar.activation(soft[a].rearrange("p (c n) -> p c n", n=CH), M.PS[:, 3 * a:3 * a + 3, 0:CH],
                                     ACT.Abs, bias=M.bg[:, a:a + 1]).then_inc(absd, 1)
            act.wait_ge(absd, 2)
            for a in range(2):
                nc.scalar.activation(soft[a], soft[a], EXP, scale=-1.0).then_inc(soft_r, 1)
            act.wait_ge(soft_r, 2)
            for a in range(2):
                nc.scalar.activation(soft[a], soft[a], ACT.Ln, bias=M.one[:, 0:1]).then_inc(soft_r, 1)
            act.wait_ge(g_ready, 2)
            nc.scalar.activation(eg.rearrange("p b a -> p a b"), gT[:, :, T:N], EXP, scale=1 / 16).then_inc(egr, 1)
            with act.Fori(0, QT) as t:
                act.wait_ge(scan, t + 1)
                nc.scalar.activation(eb, bt, EXP, scale=1 / 16)
                nc.scalar.activation(enb, bt, EXP, scale=-1 / 16).then_inc(ebr, 1)
                act.wait_ge(dlr, t + 1)
                nc.scalar.activation(dl, dl, EXP, scale=1 / 16).then_inc(edl, 1)
                act.wait_ge(orr, t + 1)
                act.wait_ge(vtd, t + 2)
                nc.scalar.activation(vtk, M.PS[:, VT, :].rearrange("p (a n) -> p a n", n=P), ACT.Copy)
                act.wait_ge(ktd, t + 1)
                nc.scalar.activation(kltk, M.PS[:, KT, 0:256].rearrange("p (a n) -> p a n", n=P), ACT.Copy)\
                  .then_inc(vke, 1)
                act.wait_ge(orr, t + 2)
                for q in range(2):
                    last = nc.scalar.activation(M.hT[:, q:4:2, ds(t * P, P)],
                                                M.PS[:, OB + q, 0:256].rearrange("p (a n) -> p a n", n=P), ACT.Copy)
                last.then_inc(oev, 1)
            for h in range(GH):
                nc.scalar.activation(M.Z[:, 4 + h, :], M.Z[:, Z_GR + h, :], ACT.Sigmoid).then_inc(den, 1)
            act.wait_ge(so, 1)
            for q in range(2):
                nc.scalar.activation(M.hT[:, q:4:2, T:N], M.PS[:, OB + q, 0:16].rearrange("p (a b) -> p a b", b=B),
                                     ACT.Copy).then_inc(soe, 1)
            act.wait_ge(soe, 2)
            for h in range(GH):
                nc.scalar.activation(M.Z[:, h, :], M.hT[:, h, :], ACT.Square).then_inc(sq, 1)
            for h in range(GH):
                act.wait_ge(ss, h + 1)
                nc.scalar.activation(M.Z[:, h, :].rearrange("p (c n) -> p c n", n=CH),
                                     M.PS[:, 3 * (h % 2):3 * (h % 2) + 3, 0:CH], ACT.Ln,
                                     bias=M.eps[:, 0:1], scale=1.0 / DV).then_inc(rt, 1)
            for h in range(GH):
                act.wait_ge(rt, h + 1)
                nc.scalar.activation(M.Z[:, h, :], M.Z[:, h, :], EXP, scale=-0.5).then_inc(rs, 1)

        @block.vector
        def _(dve):
            ch = Chain(dve, step)
            dve.wait_ge(absd, 2)
            for a in range(2):
                ch(nc.vector.tensor_scalar(gT[:, a, :].rearrange("p (c n) -> p c n", n=CH),
                                           M.PS[:, 3 * a:3 * a + 3, 0:CH], M.bg[:, a:a + 1], 0.0,
                                           ALU.add, ALU.min))
            for a in range(2):
                dve.wait_ge(soft_r, 3 + a)
                nc.vector.tensor_tensor(gT[:, a, :], gT[:, a, :], soft[a], ALU.subtract).then_inc(g_ready, 1)
            nc.vector.tensor_scalar_mul(qs, M.zs[:, Z_GQ:Z_GQ + 2, :], DK ** -0.5).then_inc(qsr, 1)
            ch(nc.vector.memset(Sa, 0.0))
            dve.wait_ge(g_ready, 2)
            dve.wait_ge(tri_r, 1)
            with dve.Fori(0, QT) as t:
                for a in range(2):
                    for c in range(2):
                        last = nc.vector.tensor_tensor_scan(
                            bt[:, a, c * CHUNK:(c + 1) * CHUNK], M.ones[:, 0:CHUNK],
                            gT[:, a, ds(t * P + c * CHUNK, CHUNK)], 0.0, ALU.mult, ALU.add)
                last.then_inc(scan, 1)
                dve.wait_ge(scan, t + 1)
                b4 = bt.rearrange("p a (c n) -> p (a c) n", n=CHUNK)
                ends = b4[:, :, CHUNK - 1:CHUNK].to_broadcast([P, 4, CHUNK])
                nc.vector.tensor_tensor(dl.rearrange("p a (c n) -> p (a c) n", n=CHUNK), ends, b4, ALU.subtract)\
                  .then_inc(dlr, 1)
                dve.wait_ge(ebr, t + 1)
                dve.wait_ge(orr, t + 1)
                nc.vector.scalar_tensor_tensor(out=qe, in0=M.Z[:, Z_GQ:Z_GQ + 2, ds(t * P, P)], scalar=DK ** -0.5,
                                               in1=eb, op0=ALU.mult, op1=ALU.mult)
                nc.vector.tensor_tensor(ke, M.Z[:, Z_GK:Z_GK + 2, ds(t * P, P)], enb, ALU.mult).then_inc(qk, 1)
                dve.wait_ge(edl, t + 1)
                nc.vector.tensor_tensor(kl, M.Z[:, Z_GK:Z_GK + 2, ds(t * P, P)], dl, ALU.mult).then_inc(klr, 1)
                dve.wait_ge(ar, t + 1)
                for q in range(2):
                    last = nc.vector.tensor_tensor(Amq[:, q, :, :],
                                                   M.PS[:, X + q, 0:256].rearrange("p (a n) -> p a n", n=P),
                                                   tri.rearrange("p (a n) -> p a n", a=1).to_broadcast([P, 2, P]),
                                                   ALU.mult)
                last.then_inc(amr, 1)
                dve.wait_ge(dsr, t + 1)
                for a in range(2):
                    last = nc.vector.scalar_tensor_tensor(
                        out=Sb[:, a, :], in0=Sa[:, a, :], scalar=eb[:, a, CHUNK - 1:CHUNK],
                        in1=M.PS[:, DS, a * P:(a + 1) * P], op0=ALU.mult, op1=ALU.add)
                last.then_inc(sbr, 1)
                dve.wait_ge(sbr, t + 1)
                dve.wait_ge(in0, t + 1)
                for a in range(2):
                    last = nc.vector.scalar_tensor_tensor(
                        out=Sa[:, a, :], in0=Sb[:, a, :], scalar=eb[:, a, P - 1:P],
                        in1=M.PS[:, DS + 1, a * P:(a + 1) * P], op0=ALU.mult, op1=ALU.add)
                last.then_inc(sar, 1)
                dve.wait_ge(sar, t + 1)
            dve.wait_ge(st_l, 16)
            dve.wait_ge(egr, 1)
            ch(nc.vector.tensor_tensor(state.rearrange("p b a v -> p (b a) v"), state.rearrange("p b a v -> p (b a) v"),
                                       eg.rearrange("p b a -> p (b a)").rearrange("p (x y) -> p x y", y=1)
                                       .to_broadcast([P, 2 * B, DV]), ALU.mult))
            for b in range(B):
                if b >= 1:
                    dve.wait_ge(vb, b)
                nc.vector.tensor_tensor(dg, M.ident[:, :].rearrange("p (a n) -> p a n", a=1).to_broadcast([P, 4, P]),
                                        M.zs[:, Z_GV:Z_GV + 4, b:b + 1].to_broadcast([P, 4, P]), ALU.mult)\
                  .then_inc(dgr, 1)
                dve.wait_ge(vb, b + 1)
                for a in range(2):
                    last = nc.vector.scalar_tensor_tensor(out=state[:, b, a, :],
                                                          in0=M.PS[:, X + b % 2, a * P:(a + 1) * P],
                                                          scalar=M.zs[:, Z_GK + a, b:b + 1], in1=state[:, b, a, :],
                                                          op0=ALU.mult, op1=ALU.add)
                last.then_inc(stn, 1)
            for h in range(GH):
                t1 = M.Z[:, 4 + h, :]
                dve.wait_ge(den, h + 1)
                ch(nc.vector.tensor_tensor(t1, t1, M.Z[:, Z_GR + h, :], ALU.mult))
                dve.wait_ge(rs, h + 1)
                ch(nc.vector.scalar_tensor_tensor(out=M.Z[:, h, :], in0=M.Z[:, h, :], scalar=M.gn[:, 0:1],
                                                  in1=t1, op0=ALU.mult, op1=ALU.mult))
                nc.vector.tensor_tensor(M.hT[:, h, :], M.hT[:, h, :], M.Z[:, h, :], ALU.mult).then_inc(mixed, 1)

        @block.tensor
        def _(pe):
            for a in range(2):
                for c in range(3):
                    last = nc.tensor.matmul(M.PS[:, 3 * a + c, 0:CH], M.wg[:, a * P:(a + 1) * P],
                                            M.Z[0:RANK, Z_SM, c * CH:(c + 1) * CH], start=True, stop=True)
                last.then_inc(xg, 1)
            pe.sem_inc(vtd, 1)
            pe.sem_inc(orr, 1)
            with pe.Fori(0, QT) as t:
                pe.wait_ge(vst, t + 1)
                for h in range(GH):
                    last = nc.tensor.transpose(M.PS[:, VT, h * P:(h + 1) * P], v_s[:, h, :], M.ident[:, :])
                last.then_inc(vtd, 1)
                pe.wait_ge(qk, t + 1)
                for a in range(2):
                    for q in range(2):
                        r = slice(q * DK, (q + 1) * DK)
                        last = nc.tensor.matmul(M.PS[:, X + q, a * P:(a + 1) * P], ke[r, a, :], qe[r, a, :],
                                                start=True, stop=True)
                last.then_inc(ar, 1)
                pe.wait_ge(klr, t + 1)
                for a in range(2):
                    last = nc.tensor.transpose(M.PS[:, KT, a * P:(a + 1) * P], kl[:, a, :], M.ident[:, :])
                last.then_inc(ktd, 1)
                pe.wait_ge(vke, t + 1)
                pe.wait_ge(amr, t + 1)
                for a in range(2):
                    for q in range(2):
                        nc.tensor.matmul(M.PS[:, OB + q, a * P:(a + 1) * P], vtk[:, 2 * a + q, :],
                                         Amq[:, q, a, :], start=(a == 0), stop=False, skip_group_check=True)
                for c in range(2):
                    for a in range(2):
                        for q in range(2):
                            last = nc.tensor.matmul(M.PS[q * DK:(q + 1) * DK, DS + c, a * P:(a + 1) * P],
                                                    kltk[c * CHUNK:(c + 1) * CHUNK, a, q * DK:(q + 1) * DK],
                                                    vtk[c * CHUNK:(c + 1) * CHUNK, 2 * a + q, :],
                                                    start=True, stop=True)
                last.then_inc(dsr, 1)

                def inter(state_, c):
                    for a in range(2):
                        for q in range(2):
                            r = slice(q * DK, (q + 1) * DK)
                            last = nc.tensor.matmul(M.PS[:, OB + q, a * P + c * CHUNK:a * P + (c + 1) * CHUNK],
                                                    state_[r, a, :], qe[r, a, c * CHUNK:(c + 1) * CHUNK],
                                                    start=False, stop=True, skip_group_check=True)
                    return last

                inter(Sa, 0).then_inc(in0, 1)
                pe.wait_ge(sbr, t + 1)
                inter(Sb, 1).then_inc(orr, 1)
            for b in range(B):
                pe.wait_ge(dgr, b + 1)
                if b >= 2:
                    pe.wait_ge(stn, b - 1)
                for q in range(2):
                    last = nc.tensor.matmul(M.PS[q * DK:(q + 1) * DK, X + b % 2, 0:256], M.ones[:, 0:DK],
                                            dg[:, q:4:2, :], start=True, stop=True)
                last.then_inc(vb, 1)
            pe.wait_ge(stn, B)
            pe.wait_ge(qsr, 1)
            pe.wait_ge(oev, QT)
            for b in range(B):
                for a in range(2):
                    for q in range(2):
                        r = slice(q * DK, (q + 1) * DK)
                        last = nc.tensor.matmul(M.PS[:, OB + q, a * B + b:a * B + b + 1], state[r, b, a, :],
                                                qs[r, a, b:b + 1], start=True, stop=True)
            last.then_inc(so, 1)
            for h in range(GH):
                pe.wait_ge(sq, h + 1)
                if h >= 2:
                    pe.wait_ge(rt, h - 1)
                for c in range(3):
                    last = nc.tensor.matmul(M.PS[:, 3 * (h % 2) + c, 0:CH], M.ones[:, :],
                                            M.Z[:, h, c * CH:(c + 1) * CH], start=True, stop=True)
                last.then_inc(ss, 1)

        @block.sync
        def _(sp):
            sp.wait_ge(sar, QT)
            sp.dma_start(O["gla_prompt"][0, 0].rearrange("(a q) k v -> (q k) a v", q=2), Sa).then_inc(stored, 16)
            sp.dma_start(state, A["state_gla"][0].rearrange("b (a q) k v -> (q k) b a v", q=2)).then_inc(st_l, 16)
            sp.wait_ge(stn, B)
            sp.dma_start(O["gla_sample"][0].rearrange("b (a q) k v -> (q k) b a v", q=2), state).then_inc(stored, 16)
            sp.wait_ge(stored, 32)


def phase_compress(nc, M, A):
    M.w1 = M.Zf[:, 0:4096].rearrange("p (v j f) -> p v j f", v=2, f=CHID)
    M.pe = M.misc[:, 192:224].rearrange("p (v j) -> p v j", v=2)
    M.w2 = M.misc[:, 224:352].rearrange("p (v d) -> p v d", v=2)
    M.hb = M.misc[:, 604:606]
    M.kcT, M.vcp = M.misc[:, 0:NCP], M.misc[:, 64:64 + P]
    hid = M.misc[:, 352:352 + 4 * NCP].rearrange("p (v h n) -> p v h n", v=2, h=2)
    x2 = M.Zf[:, 8576:8576 + 2048].rearrange("p (v h r n) -> p v h r n", v=2, h=2, r=8)
    M.slope = M.misc[:, 608:616].rearrange("p (k g) -> p k g", k=KVH)
    RS, RW, RC = M.srow[:, 0:RSEL], M.srow[:, RSEL:RSEL + RWIN], M.srow[:, RSEL + RWIN:RSEL + RWIN + RCMP]
    w_l, x2_r, conv, hidr, kv_r = (M.sem(x) for x in ("cmp_w_loaded", "cmp_x", "cmp_conv", "cmp_hid", "cmp_kv"))
    tm, hbr, slr = M.sem("template_step"), M.sem("cmp_bias"), M.sem("slopes_set")

    with nc.Block() as block:
        @block.sync
        def _(sp):
            for v, (w1, pe_, w2) in enumerate((("w_cmpk_1", "pe_cmpk", "w_cmpk_2"), ("w_cmpv_1", "pe_cmpv", "w_cmpv_2"))):
                sp.dma_start(M.w1[:, v, :, :], A[w1][0].rearrange("(j q) d f -> (q d) j f", q=2)).then_inc(w_l, 16)
                sp.dma_start(M.pe[:, v, :], A[pe_][0].rearrange("(j q) d -> (q d) j", q=2),
                             allow_slow_non_contiguous=True).then_inc(w_l, 16)
                sp.dma_start(M.w2[:, v, :], A[w2][0]).then_inc(w_l, 16)

        @block.gpsimd
        def _(pool):
            for h in range(H):
                pool.memset(M.slope[:, h // G, h % G:h % G + 1], 2.0 ** (-8.0 * (h + 1) / H)).then_inc(slr, 1)
            for r, pat, base in ((RS, [[1, RSEL]], -(T - P)), (RW, [[1, RWIN]], -WIN),
                                 (RC, [[CSTR, RCMP]], CLEN - 1 - (T - P))):
                pool.iota(r, pattern=pat, base=base, channel_multiplier=-1,
                          allow_small_or_imprecise_dtypes=True).then_inc(tm, 1)
            pool.wait_ge(tm, 3)
            for r, pat, base in ((RS, [[-1, RSEL]], T - P), (RW, [[-1, RWIN]], WIN),
                                 (RC, [[-CSTR, RCMP]], T - P - (CLEN - 1))):
                pool.affine_select(out=r, in_=r, compare_op=ALU.is_ge, fill=MASKED, base=base, pattern=pat,
                                   channel_multiplier=1).then_inc(tm, 1)
            pool.wait_ge(tm, 6)
            pool.affine_select(out=RW, in_=RW, compare_op=ALU.is_ge, fill=MASKED, base=0, pattern=[[1, RWIN]],
                               channel_multiplier=-1).then_inc(tm, 1)

        @block.vector
        def _(dve):
            for v in range(2):
                for h in range(2):
                    for q in range(2):
                        src = M.Z[h * HD:(h + 1) * HD, Z_KV + v, 0:T].rearrange("p (n r q) -> p q r n", r=8, q=2)
                        last = nc.vector.tensor_copy(x2[q * HD:(q + 1) * HD, v, h, :, :], src[:, q, :, :])
                last.then_inc(x2_r, 1)

        @block.tensor
        def _(pe):
            pe.wait_ge(w_l, 96)
            for v in range(2):
                for j in range(16):
                    last = nc.tensor.matmul(M.PS[:, 2 + v, 0:1], M.w1[:, v, j, :], M.pe[:, v, j:j + 1],
                                            start=(j == 0), stop=(j == 15))
            last.then_inc(conv, 1)
            for v in range(2):
                pe.wait_ge(x2_r, v + 1)
                for j in range(16):
                    last = nc.tensor.matmul(M.PS[:, v, 0:2 * NCP], M.w1[:, v, j, :],
                                            x2[:, v, :, j % 8, j // 8:j // 8 + NCP], start=(j == 0), stop=(j == 15))
                last.then_inc(conv, 1)
            pe.wait_ge(hidr, 2)
            for h in range(2):
                nc.tensor.matmul(M.PS[h * HD:(h + 1) * HD, 4, 0:NCP], M.w2[:, 0, :], hid[:, 0, h, :],
                                 start=True, stop=True)
            for h in range(2):
                last = nc.tensor.matmul(M.PS[0:NCP, 5, h * HD:(h + 1) * HD], hid[:, 1, h, :], M.w2[:, 1, :],
                                        start=True, stop=True)
            last.then_inc(kv_r, 1)

        @block.scalar
        def _(act):
            act.wait_ge(conv, 1)
            nc.scalar.activation(M.hb, M.PS[:, 2:4, 0], ACT.Copy).then_inc(hbr, 1)
            act.wait_ge(hbr, 1)
            for v in range(2):
                act.wait_ge(conv, v + 2)
                nc.scalar.activation(hid[:, v, :, :].rearrange("p h n -> p (h n)"), M.PS[:, v, 0:2 * NCP],
                                     ACT.Gelu_apprx_tanh, bias=M.hb[:, v:v + 1]).then_inc(hidr, 1)
            act.wait_ge(kv_r, 1)
            nc.scalar.activation(M.kcT, M.PS[:, 4, 0:NCP], ACT.Copy)
            nc.scalar.activation(M.vcp[0:NCP, :], M.PS[0:NCP, 5, 0:P], ACT.Copy)


def phase_attend(nc, M):
    RT = RSEL + RWIN + RCMP
    q_s = M.Zf[:, 4096:4096 + T]
    W = T + RWIN + 64
    sbuf = M.Zf[:, 5120:5120 + 2 * W].rearrange("p (s w) -> p s w", s=2)
    pt = M.Zf[:, 8576:8576 + 2 * 14 * P].rearrange("p (s w) -> p s w", s=2)
    RB = [M.srow[:, RT:2 * RT], M.ring[:, 2048:2048 + RT]]
    ytok = M.misc[:, 616:616 + 2 * P].rearrange("p (s c) -> p s c", s=2)
    neg = M.misc[:, 880:888].rearrange("p (s c) -> p s c", s=2)
    mx = M.misc[:, 888:896].rearrange("p (s c) -> p s c", s=2)
    sm = M.misc[:, 896:904].rearrange("p (s c) -> p s c", s=2)
    rc = M.misc[:, 904:912].rearrange("p (s c) -> p s c", s=2)
    PSf = M.PS[:, :, :].rearrange("p b n -> p (b n)")
    CMP0, WIN0, SEL0 = T + RWIN, T, 0
    U = 2 * QT

    def shape(u):
        qt, kvh = u // 2, u % 2
        j0 = max(0, qt - WIN // P)
        return qt, kvh, j0, (qt + 1) * P, (qt - j0 + 1) * P

    def tiles(u):
        qt, _, j0, ls, lw = shape(u)
        t = [(WIN0 + c, P) for c in range(0, lw, P)] + [(SEL0 + c, P) for c in range(0, ls, P)]
        return t[:3] + [(CMP0, NCP)] + t[3:]

    def groups(u):
        t = tiles(u)
        return [t[g:g + 4] for g in range(0, len(t), 4)]

    first = [sum(len(groups(v)) for v in range(u)) for u in range(U + 1)]
    NG = first[U]
    assert NG % 2 == 0
    q_r, rb_r = M.sem("q_slot"), M.sem("rb_ready")
    scores, sread, maxr, probs = M.sem("scores"), M.sem("scores_read"), M.sem("max_ready"), M.sem("probs")
    turned, ptm, pv, merged = M.sem("p_turned"), M.sem("p_moved"), M.sem("pv_done"), M.sem("merged")
    yt, ym, step = M.sem("y_turned"), M.sem("y_moved"), M.sem("merge_step")
    passed = M.sem("attend_passed")
    per = 7 * U

    with nc.Block() as block:
        @block.gpsimd
        def _(pool):
            with pool.Fori(0, G) as hh:
                pool.wait_ge(sread, hh * U + 1)
                for kvh in range(KVH):
                    last = pool.tensor_tensor(RB[kvh], M.srow[:, 0:RT],
                                              M.slope[:, kvh, ds(hh, 1)].to_broadcast([P, RT]), ALU.mult)
                last.then_inc(rb_r, 1)

        @block.scalar
        def _(act):
            def exps(hh, u):
                qt, kvh, j0, ls, lw = shape(u)
                s = u % 2
                act.wait_ge(maxr, hh * U + (u + 1))
                for br, (c, w) in enumerate(((CMP0, NCP), (SEL0, ls), (WIN0, lw))):
                    last = nc.scalar.activation(sbuf[:, s, c:c + w], sbuf[:, s, c:c + w], ACT.Exp,
                                                bias=neg[:, s, br:br + 1], accum_out=sm[:, s, br:br + 1])
                last.then_inc(probs, 1)

            def y_out(hh, qt):
                act.wait_ge(yt, hh * QT + (qt + 1))
                nc.scalar.activation(M.hT[:, ds(hh + 4, 1), qt * P:(qt + 1) * P],
                                     M.PS[:, 7:8, 256:384], ACT.Copy).then_inc(ym, 1)

            with act.Fori(0, G) as hh:
                nc.scalar.activation(q_s, M.Z[:, ds(hh + Z_Q, 1), 0:T].rearrange("p a n -> p (a n)"), ACT.Copy,
                                     scale=HD ** -0.5).then_inc(q_r, 1)
                exps(hh, 0)
                for u in range(U):
                    for g, grp in enumerate(groups(u)):
                        act.wait_ge(turned, hh * NG + (first[u] + g + 1))
                        if g == 0:
                            act.wait_ge(pv, hh * U + (u + 1))
                        o, bank = g * 4 * P, M.PS[:, 4 + (first[u] + g) % 2, :]
                        n = (len(grp) - (g == 0)) * P
                        last = nc.scalar.activation(pt[:, u % 2, o:o + n], bank[:, 0:n], ACT.Copy)
                        if g == 0:
                            last = nc.scalar.activation(pt[0:NCP, u % 2, n:n + P], bank[0:NCP, n:n + P], ACT.Copy)
                        last.then_inc(ptm, 1)
                    if u + 1 < U:
                        exps(hh, u + 1)
                    if u % 2 == 0 and u >= 2:
                        y_out(hh, u // 2 - 1)
                y_out(hh, QT - 1)

        @block.vector
        def _(dve):
            ch = Chain(dve, step)
            dve.sem_inc(sread, 1)
            dve.sem_inc(merged, 2)

            def score(hh, u):
                qt, kvh, j0, ls, lw = shape(u)
                s = u % 2
                dve.wait_ge(scores, hh * U + (u + 1))
                if u >= 2:
                    dve.wait_ge(turned, hh * NG + first[u - 1])
                offs = ((CMP0, NCP, RSEL + RWIN + (T - P) // CSTR - qt * P // CSTR), (SEL0, ls, T - P - qt * P),
                        (WIN0, lw, RSEL + (j0 - qt) * P + WIN))
                dve.sem_inc(passed, 1)
                for br, (c, w, r) in enumerate(offs):
                    last = nc.vector.tensor_tensor_reduce(out=sbuf[:, s, c:c + w], in0=PSf[:, c:c + w],
                                                          in1=RB[kvh][:, r:r + w], scale=1.0, scalar=FLOOR,
                                                          op0=ALU.add, op1=ALU.max, accum_out=mx[:, s, br:br + 1])
                last.then_inc(sread, 1)
                dve.wait_ge(sread, hh * U + (u + 2))
                nc.vector.tensor_scalar_mul(neg[:, s, 0:3], mx[:, s, 0:3], -1.0).then_inc(maxr, 1)

            def merge(hh, u):
                qt, kvh = u // 2, u % 2
                s = u % 2
                dve.wait_ge(probs, hh * U + (u + 1))
                ch(nc.vector.tensor_scalar_max(rc[:, s, 0:3], sm[:, s, 0:3], 1e-30))
                ch(nc.vector.reciprocal(rc[:, s, 0:3], rc[:, s, 0:3]))
                gates = M.gt[:, qt, :].rearrange("p (b h) -> p b h", b=3)[:, :, ds(hh + G * kvh, 1)]
                ch(nc.vector.tensor_tensor(rc[:, s, 0:3].rearrange("p (b h) -> p b h", h=1),
                                           rc[:, s, 0:3].rearrange("p (b h) -> p b h", h=1), gates, ALU.mult))
                dve.wait_ge(pv, hh * U + (u + 3))
                y = ytok[:, qt % 2, kvh * HD:(kvh + 1) * HD]
                if kvh == 0 and qt >= 2:
                    dve.wait_ge(yt, hh * QT + (qt - 1))
                o = M.PS[:, 6 + kvh, 0:3 * HD].rearrange("p (b d) -> p b d", b=3)
                ch(nc.vector.tensor_scalar_mul(y, o[:, 0, :], rc[:, s, 0:1]))
                ch(nc.vector.scalar_tensor_tensor(out=y, in0=o[:, 1, :], scalar=rc[:, s, 1:2], in1=y,
                                                  op0=ALU.mult, op1=ALU.add))
                last = nc.vector.scalar_tensor_tensor(out=y, in0=o[:, 2, :], scalar=rc[:, s, 2:3], in1=y,
                                                      op0=ALU.mult, op1=ALU.add)
                last.then_inc(merged, 1)

            with dve.Fori(0, G) as hh:
                ch.enter(hh, 5 * U)
                dve.wait_ge(rb_r, hh + 1)
                score(hh, 0)
                for u in range(U):
                    if u + 1 < U:
                        score(hh, u + 1)
                    merge(hh, u)
            ch.leave(G)

        @block.tensor
        def _(pe):
            pe.sem_inc(pv, 2)

            def score(hh, u):
                qt, kvh, j0, ls, lw = shape(u)
                r = slice(kvh * HD, (kvh + 1) * HD)
                pe.wait_ge(sread, hh * U + (u + 1))
                lhsT = q_s[r, qt * P:(qt + 1) * P]
                for c in range(0, ls, 512):
                    n = min(512, ls - c)
                    nc.tensor.matmul(PSf[:, c:c + n], lhsT, M.Z[r, Z_KV + 2, c:c + n], start=True, stop=True)
                for c in range(0, lw, 512):
                    n = min(512, lw - c)
                    nc.tensor.matmul(PSf[:, WIN0 + c:WIN0 + c + n], lhsT,
                                     M.Z[r, Z_KV + 4, j0 * P + c:j0 * P + c + n], start=True, stop=True)
                nc.tensor.matmul(PSf[:, CMP0:CMP0 + NCP], lhsT, M.kcT[r, :], start=True, stop=True)\
                  .then_inc(scores, 1)

            def values(hh, u):
                qt, kvh, j0, ls, lw = shape(u)
                s = u % 2
                pe.wait_ge(probs, hh * U + (u + 1))
                for g, grp in enumerate(groups(u)):
                    if first[u] + g >= 2:
                        pe.wait_ge(ptm, hh * NG + (first[u] + g - 1))
                    for n, (c, w) in enumerate(grp):
                        last = nc.tensor.transpose(M.PS[0:w, 4 + (first[u] + g) % 2, n * P:(n + 1) * P],
                                                   sbuf[:, s, c:c + w], M.ident[:, :])
                    last.then_inc(turned, 1)
                if u % 2 == 0 and u >= 2:
                    y_turn(hh, u // 2 - 1)
                pe.wait_ge(ptm, hh * NG + first[u + 1])
                pe.wait_ge(merged, hh * U + (u + 1))
                if u == 1:
                    pe.wait_ge(ym, hh * QT + 1)
                elif u % 2 == 1:
                    pe.wait_ge(ym, hh * QT + (u // 2 + 1))
                bank = M.PS[:, 6 + kvh, :]
                d = slice(kvh * HD, (kvh + 1) * HD)
                nw, ns = lw // P, ls // P
                at = [c for c, _ in tiles(u)]

                def p_of(c):
                    return pt[:, s, at.index(c) * P:(at.index(c) + 1) * P]

                nc.tensor.matmul(bank[:, 0:HD], p_of(CMP0)[0:NCP, :], M.vcp[0:NCP, d], start=True, stop=True)
                for n in range(ns):
                    nc.tensor.matmul(bank[:, HD:2 * HD], p_of(SEL0 + n * P),
                                     M.vtok[:, n, 0, d], start=(n == 0), stop=(n == ns - 1))
                for n in range(nw):
                    last = nc.tensor.matmul(bank[:, 2 * HD:3 * HD], p_of(WIN0 + n * P),
                                            M.vtok[:, j0 + n, 1, d], start=(n == 0), stop=(n == nw - 1))
                last.then_inc(pv, 1)

            def y_turn(hh, qt):
                pe.wait_ge(merged, hh * U + (2 * qt + 4))
                nc.tensor.transpose(M.PS[:, 7, 256:384], ytok[:, qt % 2, :], M.ident[:, :]).then_inc(yt, 1)

            pe.sem_inc(ym, 1)
            with pe.Fori(0, G) as hh:
                pe.wait_ge(q_r, hh + 1)
                score(hh, 0)
                for u in range(U):
                    if u + 1 < U:
                        score(hh, u + 1)
                    values(hh, u)
                y_turn(hh, QT - 1)


def phase_sample_setup(nc, M, A, O):
    M.bias = M.ring[0:H, :].rearrange("h (q m) -> h q m", q=2)
    small = M.misc[:, 2200:2560]
    M.pages = M.wg[0:1, :].bitcast(INT32)
    M.sl8, M.gsum, M.qb, M.newk = small[0:H, 0:1], small[0:H, 1:9], small[:, 9:17], small[:, 17:19]
    M.qbs = M.misc[:, 2368:2376]
    M.vn = M.Zf[0:1, 22720:24768].rearrange("p (w b x) -> p w b x", w=2, x=P)
    bs, sl, gs, bz = M.sem("bias_steps"), M.sem("slope_col"), M.sem("gsum_steps"), M.sem("qb_zeroed")
    with nc.Block() as block:
        @block.sync
        def _(sp):
            sp.dma_start(M.sl8, M.slope[0:1, :, :].rearrange("p k (g x) -> p (k g) x", x=1)).then_inc(sl, 16)
            sp.dma_start(M.pages, A["page_table"].rearrange("b n -> (b n)").rearrange("(a n) -> a n", a=1))\
              .then_inc(sl, 16)
            sp.dma_start(M.vn[:, 0, :, :], O["kv_sample"][:, :, 0, 3].rearrange("a b h d -> a b (h d)")).then_inc(sl, 16)
            sp.dma_start(M.vn[:, 1, :, :], O["win_sample"][:, :, WIN - 1, 1].rearrange("a b h d -> a b (h d)"))              .then_inc(sl, 16)
            sp.wait_ge(sl, 64)

        @block.gpsimd
        def _(pool):
            pool.iota(M.bias, pattern=[[1, 2], [2, PAST // 2]], base=-PAST, channel_multiplier=0,
                      allow_small_or_imprecise_dtypes=True).then_inc(bs, 1)
            pool.memset(M.gsum, 1.0).then_inc(gs, 1)
            g2 = M.gsum.rearrange("p (g x) -> p g x", g=KVH)
            pool.wait_ge(gs, 1)
            pool.affine_select(out=g2, in_=g2, compare_op=ALU.is_ge, fill=0.0, base=0,
                               pattern=[[-G, KVH], [0, G]], channel_multiplier=1).then_inc(gs, 1)
            pool.wait_ge(gs, 2)
            pool.affine_select(out=g2, in_=g2, compare_op=ALU.is_ge, fill=0.0, base=G - 1,
                               pattern=[[G, KVH], [0, G]], channel_multiplier=-1).then_inc(gs, 1)
            pool.memset(M.qb, 0.0)
            pool.memset(M.qbs, 0.0).then_inc(bz, 1)

        @block.vector
        def _(dve):
            dve.wait_ge(bs, 1)
            dve.wait_ge(sl, 64)
            nc.vector.tensor_scalar(M.bias, M.bias, M.sl8, None, ALU.mult)
            nc.vector.memset(M.misc[0:H, 1126 + NCS:1126 + 256], 0.0)


def phase_sample(nc, M, A, O):
    NT = NPAGES // 2
    NS, SEG = 4, NT // 2
    SG = SEG * P // (CSTR // 2)
    HALF = PAST // 2
    Zf = M.Zf
    raw = Zf[:, 4096:8192].rearrange("p (s q w x) -> p s q w x", s=NS, q=2, w=4)
    stage = Zf[:, 8192:9216].rearrange("p (s w q d) -> p s w q d", s=2, w=4, q=2)
    x2 = Zf[:, 9216:9216 + 8 * 8 * (SG + 1)].rearrange("p (g w r n) -> p g w r n", g=2, w=4, r=8)
    kslT = Zf[:, 17472:21568].rearrange("p (q m) -> p q m", q=2)
    wraw = Zf[:, 21568:22592].rearrange("p (c x) -> p c x", c=4)
    vslc = M.X[:, :, :].rearrange("p a n -> p (a n)")\
        .rearrange("p (b i q x) -> p b i q x", b=2, i=NT, q=2)
    s = M.srow[0:H, 0:PAST + 1]
    sq = s[:, 0:PAST].rearrange("h (q m) -> h q m", q=2)
    sraw = M.srow[32:32 + H, 0:PAST].rearrange("h (q m) -> h q m", q=2)
    hid = M.misc[:, 616:616 + 2 * NCS].rearrange("p (h n) -> p h n", h=2)
    kcT, pc = M.misc[:, 1126:1126 + NCS], M.misc[0:H, 1126:1126 + 256]
    kwT, sw = M.misc[:, 1382:1382 + WIN], M.misc[0:H, 1382:1382 + WIN + 1]
    pT = M.misc[:, 1896:1896 + 304]
    vc = [M.misc[:, 0:P], M.misc[:, 2240:2240 + P]]
    sc = M.misc[0:H, 2496:2560]
    top = sc[:, 0:8]
    neg, sm, mx, rcp = sc[:, 8:12], sc[:, 12:16], sc[:, 16:20], sc[:, 20:24]
    y8 = M.misc[0:H, 1382:1382 + P]
    spare = M.gt[:, :, :].rearrange("p t g -> p (t g)")
    imp, pen = M.misc[0:H, 2376:2376 + NSELS], spare[32:32 + H, 0:NSELS]
    vn = [M.misc[0:1, 352:352 + P], spare[0:1, 0:P]]
    S = M.sem
    ld = [S(f"tile_slot{i}_loaded") for i in range(NS)]
    wl, stg, trn, cmpm, slm, vcp, edge = (S(x) for x in (
        "win_loaded", "tile_staged", "tile_turned", "cmp_moved", "slc_moved", "vslc_copied", "edge_copied"))
    qsr, qbr, qkd, qkm, nwd, nwm = (S(x) for x in (
        "q_next_ready", "q_ready", "qk_done", "qk_moved", "new_done", "new_moved"))
    kwt, kwm, qwd, swm = S("kw_turned"), S("kw_moved"), S("qk_win_done"), S("win_max")
    cvd, gel, kcd, kcv = S("conv_done"), S("gelu_done"), S("kc_done"), S("kc_moved")
    qcd, cmx, exc, impr = S("qk_cmp_done"), S("cmp_max"), S("cmp_exp"), S("imp_ready")
    gsd, gsr, smx, exs, exw = S("imp_summed"), S("imp_read"), S("sel_max"), S("sel_exp"), S("win_exp")
    vcd, vcv, ptd, ptm = S("vc_done"), S("vc_moved"), S("sample_p_turned"), S("sample_p_moved")
    pvd, y8r, y8t, y8m, step = S("sample_pv"), S("y8_ready"), S("y8_turned"), S("y8_moved"), S("sample_step")
    pasv, pasp = S("sample_passed_dve"), S("sample_passed_pe")
    cache = A["cache_nsa_kv"][0].rearrange("g (m q) w h d -> g m (q w h d)", q=2)
    npool = A["cache_nsa_kv"].shape[1]
    KB, VB, TB, SB, QB, AB, DB = 0, 1, 2, 4, 5, 6, 7

    with nc.Block() as block:
        @block.sync
        def _(sp):
            def load(n, i):
                sp.wait_ge(trn, n * NT + (i + 1))
                sp.wait_ge(vcp, n * NT + (i + 1))
                for half in range(2):
                    page = sp.value_load(M.pages[0:1, ds(n * NPAGES + (2 * i + half), 1)], min_val=0,
                                         max_val=npool - 1)
                    sp.dma_start(raw[half * 64:half * 64 + 64, i % NS].rearrange("p q w x -> p (q w x)"),
                                 cache[ds(page, 1)].rearrange("g m c -> (g m) c")).then_inc(ld[i % NS], 16)

            def load_win(b):
                sp.wait_ge(pvd, b + 1)
                sp.dma_start(wraw, A["state_nsa_win"][0, ds(b, 1)].rearrange("b (c p) w h d -> p (b c) (w h d)", p=P))\
                  .then_inc(wl, 16)

            for i in range(NT):
                load(0, i)
            with sp.Fori(0, B - 1) as b:
                for i in range(NT):
                    load(b + 1, i)
                    if i == NS:
                        load_win(b)
            load_win(B - 1)

        @block.gpsimd
        def _(pool):
            def put(n, i):
                pool.wait_ge(ld[i % NS], n * 128 + 32 * (i // NS + 1))
                pool.wait_ge(trn, n * NT + (i + 3))
                out = stage[:, i % 2].rearrange("p w q d -> p q w d")
                src = raw[:, i % NS, :, 0:2, :].rearrange("p q w (h d) -> p q (w h) d", h=2)
                one = M.one[:, :].rearrange("p (q h d) -> p q h d", q=1, h=1).to_broadcast([P, 2, 4, HD])
                pool.tensor_tensor(out, src, one, ALU.mult).then_inc(stg, 1)

            for i in range(NT):
                put(0, i)
            with pool.Fori(0, B - 1) as b:
                for i in range(NT):
                    put(b + 1, i)

        @block.tensor
        def _(pe):
            pe.sem_inc(trn, NS)
            pe.sem_inc(pvd, 1)
            id8 = M.ident[0:H, 0:H]

            def turn(n, i):
                pe.wait_ge(stg, n * NT + (i + 1))
                pe.wait_ge(cmpm, n * NT + (i + 1))
                for w in range(4):
                    nc.tensor.transpose(M.PS[:, TB + i % 2, w * P:(w + 1) * P],
                                        stage[:, i % 2, w].rearrange("p q d -> p (q d)"), M.ident[:, :])
                pe.wait_ge(slm, n * NT + (i + 2))
                for q in range(2):
                    last = nc.tensor.transpose(M.PS[:, SB, q * P:(q + 1) * P], raw[:, i % NS, q, 2, :], M.ident[:, :])
                last.then_inc(trn, 1)

            def conv(n, seg, k):
                v = k // 4
                if k == 0:
                    pe.wait_ge(cmpm, n * NT + (SEG * (seg + 1) + 2))
                    if seg == 1:
                        pe.wait_ge(edge, n + 1)
                if seg == 0 and k % 4 == 0:
                    pe.wait_ge(gel, 2 * n + (v + 1))
                out = M.PS[:, (KB, VB)[v], :].rearrange("p (h n) -> p h n", h=2)
                out = out[:, :, SG - 1:NCS] if seg else out[:, :, 0:SG - 1]
                for j in range(4 * (k % 4), 4 * (k % 4) + 4):
                    lo = j // 8 + 1 - seg
                    last = nc.tensor.matmul(out, M.w1[:, v, j, :], x2[:, seg, 2 * v:2 * v + 2, j % 8,
                                                                      lo:lo + SG - 1 + seg],
                                            start=(j == 0), stop=(j == 15))
                if seg == 1 and k % 4 == 3:
                    last.then_inc(cvd, 1)

            def qk(n, k):
                if k == 0:
                    pe.wait_ge(qsr, n + 1)
                pe.wait_ge(slm, n * NT + (4 * (k // 2) + 6))
                pe.wait_ge(qkm, n * 8 + (k + 1))
                c = k // 2 * 512
                nc.tensor.matmul(M.PS[0:H, QB, :], M.qbs, kslT[:, k % 2, c:c + 512], start=True, stop=True)\
                  .then_inc(qkd, 1)

            def tail(b, i):
                if i == 0:
                    pe.wait_ge(qbr, b + 1)
                    pe.wait_ge(y8r, b + 1)
                    for n in range(2):
                        last = nc.tensor.matmul(M.PS[0:H, DB, n:n + 1], M.qb, M.newk[:, n:n + 1],
                                                start=True, stop=True)
                    last.then_inc(nwd, 1)
                if i < 3:
                    qk(b, 5 + i)
                if i == 3:
                    pe.wait_ge(wl, b * 16 + 16)
                    pe.wait_ge(y8m, b + 1)
                    for c in range(4):
                        last = nc.tensor.transpose(M.PS[:, AB, c * P:(c + 1) * P], wraw[:, c, 0:P], M.ident[:, :])
                    last.then_inc(kwt, 1)
                if i == 4:
                    pe.wait_ge(kwm, b + 1)
                    pe.wait_ge(nwm, b + 1)
                    nc.tensor.matmul(M.PS[0:H, DB, :], M.qb, kwT, start=True, stop=True).then_inc(qwd, 1)
                if i == 5:
                    pe.wait_ge(gel, 2 * b + 3)
                    for h in range(2):
                        last = nc.tensor.matmul(M.PS[h * HD:(h + 1) * HD, AB, 0:NCS], M.w2[:, 0, :], hid[:, h, :],
                                                start=True, stop=True)
                    last.then_inc(kcd, 1)
                if i == 6:
                    pe.wait_ge(kcv, b + 1)
                    pe.wait_ge(swm, b + 1)
                    nc.tensor.matmul(M.PS[0:H, DB, 0:NCS], M.qb, kcT, start=True, stop=True).then_inc(qcd, 1)
                if i == 9:
                    pe.wait_ge(impr, b + 1)
                    pe.sem_inc(pasp, 1)
                    nc.tensor.matmul(M.PS[0:H, DB, 0:64], M.gsum, imp[:, 0:64], start=True, stop=True)\
                      .then_inc(gsd, 1)
                    pe.wait_ge(gel, 2 * b + 4)
                    for n in range(2):
                        w = min(P, NCS - n * P)
                        for h in range(2):
                            last = nc.tensor.matmul(M.PS[0:w, AB, n * P + h * HD:n * P + (h + 1) * HD],
                                                    hid[:, h, n * P:n * P + w], M.w2[:, 1, :], start=True, stop=True)
                    last.then_inc(vcd, 1)
                if i == 12:
                    pe.wait_ge(exw, b + 1)
                    pe.wait_ge(vcv, b + 1)
                    pe.sem_inc(pasp, 1)
                    for c in range(4):
                        nc.tensor.transpose(M.PS[:, AB, 256 + c * H:256 + (c + 1) * H], sw[:, c * P:(c + 1) * P], id8)
                    nc.tensor.transpose(M.PS[0:1, AB, 312:312 + H], sw[:, WIN:WIN + 1], id8)
                    for n in range(2):
                        w = min(P, NCS - n * P)
                        nc.tensor.transpose(M.PS[0:w, AB, 288 + n * H:288 + (n + 1) * H], pc[:, n * P:n * P + w], id8)
                if i == 14:
                    pe.wait_ge(exs, b + 1)
                    pe.sem_inc(pasp, 1)
                    for c in range(2 * NT):
                        nc.tensor.transpose(M.PS[:, AB, c * H:(c + 1) * H], s[:, c * P:(c + 1) * P], id8)
                    nc.tensor.transpose(M.PS[0:1, AB, 304:304 + H], s[:, PAST:PAST + 1], id8).then_inc(ptd, 1)
                if i == 15:
                    pe.wait_ge(ptm, b + 1)
                    pe.wait_ge(vcp, b * NT + (NT + NS))
                    pe.wait_ge(gsr, b + 1)
                    o = M.PS[0:H, DB, :]
                    for c in range(2 * NT):
                        nc.tensor.matmul(o[:, P:2 * P], pT[:, c * H:(c + 1) * H],
                                         vslc[:, ds(b % 2, 1), c % NT, c // NT, :].rearrange("p a x -> p (a x)"),
                                         start=(c == 0), stop=False)
                    nc.tensor.matmul(o[:, P:2 * P], M.pn[:, 0:H], vn[0], start=False, stop=True)
                    for c in range(4):
                        nc.tensor.matmul(o[:, 2 * P:3 * P], pT[:, 256 + c * H:256 + (c + 1) * H], wraw[:, c, P:2 * P],
                                         start=(c == 0), stop=False)
                    nc.tensor.matmul(o[:, 2 * P:3 * P], M.pn[:, H:2 * H], vn[1], start=False, stop=True)
                    for n in range(2):
                        w = min(P, NCS - n * P)
                        last = nc.tensor.matmul(o[:, 0:P], pT[0:w, 288 + n * H:288 + (n + 1) * H], vc[n][0:w, :],
                                                start=(n == 0), stop=(n == 1))
                    last.then_inc(pvd, 1)
                    pe.wait_ge(y8r, b + 2)
                    pe.sem_inc(pasp, 1)
                    nc.tensor.transpose(M.PS[:, AB, 320:320 + H], y8, id8).then_inc(y8t, 1)

            def ahead(n, i):
                if i >= SEG:
                    conv(n, 0, i - SEG)
                if i >= 11:
                    qk(n, i - 11)

            for i in range(NT):
                turn(0, i)
                ahead(0, i)
            with pe.Fori(0, B - 1) as b:
                for i in range(NT):
                    turn(b + 1, i)
                    if i < SEG:
                        conv(b, 1, i)
                    tail(b, i)
                    ahead(b + 1, i)
            for i in range(NT):
                if i < SEG:
                    conv(B - 1, 1, i)
                tail(B - 1, i)

        @block.scalar
        def _(act):
            act.sem_inc(y8m, 1)
            act.sem_inc(cmpm, 2)
            act.sem_inc(gel, 2)

            def move(n, i):
                act.wait_ge(trn, n * NT + (i + NS + 1))
                g, c = i // SEG, 1 + i % SEG * 16
                nc.scalar.activation(x2[:, g, :, :, c:c + 16],
                                     M.PS[:, TB + i % 2, :].rearrange("p (w n r) -> p w r n", w=4, r=8),
                                     ACT.Copy).then_inc(cmpm, 1)
                if i == SEG:
                    act.wait_ge(cmpm, n * NT + (SEG + 2))
                    nc.scalar.activation(x2[:, 1, :, :, 0:1], x2[:, 0, :, :, SG:SG + 1], ACT.Copy).then_inc(edge, 1)

            def gelu(b, v):
                act.wait_ge(cvd, 2 * b + (v + 1))
                nc.scalar.activation(hid, M.PS[:, (KB, VB)[v], :].rearrange("p (h n) -> p h n", h=2)[:, :, 0:NCS],
                                     ACT.Gelu_apprx_tanh, bias=M.hb[:, v:v + 1]).then_inc(gel, 1)

            def tail(b, i):
                if i == 3:
                    act.wait_ge(kwt, b + 1)
                    nc.scalar.activation(kwT, M.PS[:, AB, :], ACT.Copy).then_inc(kwm, 1)
                if i == 4:
                    gelu(b, 0)
                if i == 5:
                    act.wait_ge(kcd, b + 1)
                    nc.scalar.activation(kcT, M.PS[:, AB, 0:NCS], ACT.Copy).then_inc(kcv, 1)
                if i == 6:
                    act.wait_ge(swm, b + 1)
                    nc.scalar.activation(sw, sw, ACT.Exp, bias=neg[:, 2:3], accum_out=sm[:, 2:3]).then_inc(exw, 1)
                if i == 7:
                    act.wait_ge(cmx, b + 1)
                    nc.scalar.activation(pc[:, 0:NCS], pc[:, 0:NCS], ACT.Exp, bias=neg[:, 0:1],
                                         accum_out=sm[:, 0:1]).then_inc(exc, 1)
                if i == 8:
                    gelu(b, 1)
                if i == 10:
                    act.wait_ge(vcd, b + 1)
                    for n in range(2):
                        w = min(P, NCS - n * P)
                        last = nc.scalar.activation(vc[n][0:w, :], M.PS[0:w, AB, n * P:(n + 1) * P], ACT.Copy)
                    for w in range(2):
                        nc.scalar.activation(vn[w], M.vn[:, w, ds(b, 1), :].rearrange("p a x -> p (a x)"), ACT.Copy)
                    last.then_inc(vcv, 1)
                if i == 12:
                    act.wait_ge(smx, b + 1)
                    nc.scalar.activation(s[:, 0:HALF], s[:, 0:HALF], ACT.Exp, bias=neg[:, 1:2], accum_out=sm[:, 1:2])
                if i == 13:
                    nc.scalar.activation(s[:, HALF:], s[:, HALF:], ACT.Exp, bias=neg[:, 1:2], accum_out=sm[:, 3:4])\
                      .then_inc(exs, 1)
                if i == 15:
                    act.wait_ge(ptd, b + 1)
                    w = NCS - P
                    nc.scalar.activation(pT[:, 0:296], M.PS[:, AB, 0:296], ACT.Copy)
                    nc.scalar.activation(pT[0:w, 296:304], M.PS[0:w, AB, 296:304], ACT.Copy)
                    nc.scalar.activation(M.pn[:, :], M.PS[0:1, AB, 304:320], ACT.Copy).then_inc(ptm, 1)
                    act.wait_ge(y8t, b + 1)
                    for k in range(KVH):
                        r = slice(k * HD, (k + 1) * HD)
                        last = nc.scalar.activation(M.hT[r, 4:8, ds(T + b, 1)].rearrange("p a n -> p (a n)"),
                                                    M.PS[r, AB, 320 + k * G:320 + (k + 1) * G], ACT.Copy)
                    last.then_inc(y8m, 1)

            for i in range(NT):
                move(0, i)
            with act.Fori(0, B - 1) as b:
                for i in range(NT):
                    move(b + 1, i)
                    tail(b, i)
            for i in range(NT):
                tail(B - 1, i)

        @block.vector
        def _(dve):
            ch = Chain(dve, step)
            dve.sem_inc(y8r, 1)
            dve.sem_inc(slm, 2)
            dve.sem_inc(qkm, 1)
            dve.sem_inc(vcp, NS)

            def queries(out, n):
                for k in range(KVH):
                    r = slice(k * HD, (k + 1) * HD)
                    last = nc.vector.tensor_scalar(out[r, k * G:(k + 1) * G].rearrange("p (a n) -> p a n", n=1),
                                                   M.zs[r, Z_Q:Z_Q + 4, ds(n, 1)], HD ** -0.5, None, ALU.mult)
                return last

            def move(n, i, head=False):
                dve.wait_ge(ld[i % NS], n * 128 + 32 * (i // NS + 1))
                if i == 0 and not head:
                    dve.wait_ge(pvd, n)
                nc.vector.tensor_copy(vslc[:, ds(n % 2, 1), i, :, :].rearrange("p a q x -> p (a q) x"),
                                      raw[:, i % NS, :, 3, :]).then_inc(vcp, 1)
                dve.wait_ge(trn, n * NT + (i + NS + 1))
                nc.vector.tensor_copy(kslT[:, :, i * P:(i + 1) * P],
                                      M.PS[:, SB, 0:256].rearrange("p (q m) -> p q m", q=2))\
                  .then_inc(slm, 1)

            def qk(n, k):
                dve.wait_ge(qkd, n * 8 + (k + 1))
                part = slice(k // 2 * 512, k // 2 * 512 + 512)
                nc.vector.tensor_tensor(sraw[:, k % 2, part], M.PS[0:H, QB, :], M.bias[:, k % 2, part], ALU.add)\
                  .then_inc(qkm, 1)

            def mask(q):
                return nc.vector.tensor_tensor_reduce(
                    out=sq[:, q, :].rearrange("h (s m) -> h s m", m=SELB // 2),
                    in0=sraw[:, q, :].rearrange("h (s m) -> h s m", m=SELB // 2),
                    in1=pen[:, 0:64].rearrange("h (s m) -> h s m", m=1).to_broadcast([H, 64, SELB // 2]),
                    scale=1.0, scalar=FLOOR, op0=ALU.add, op1=ALU.max, accum_out=mx[:, q:q + 1])

            def tail(b, i):
                if i == 0:
                    queries(M.qb, b)
                    nc.vector.tensor_copy(M.newk.rearrange("p (a n) -> p a n", n=1),
                                          M.zs[:, Z_KV + 2:Z_KV + 5:2, ds(b, 1)]).then_inc(qbr, 1)
                if i < 3:
                    qk(b, 5 + i)
                if i == 1:
                    dve.wait_ge(nwd, b + 1)
                    nc.vector.tensor_copy(s[:, PAST:PAST + 1], M.PS[0:H, DB, 0:1])
                    nc.vector.tensor_copy(mx[:, 2:3], M.PS[0:H, DB, 0:1])
                    nc.vector.tensor_copy(rcp[:, 3:4], M.PS[0:H, DB, 1:2]).then_inc(nwm, 1)
                if i == 5:
                    dve.wait_ge(qwd, b + 1)
                    nc.vector.tensor_copy(sw[:, WIN:WIN + 1], rcp[:, 3:4])
                    ch(nc.vector.tensor_tensor(sw[:, 0:WIN].rearrange("h (m q) -> h m q", q=2),
                                               M.PS[0:H, DB, :].rearrange("h (m q) -> h m q", q=2),
                                               M.bias[:, :, HALF - WIN // 2:HALF].rearrange("h q m -> h m q"), ALU.add))
                    ch(nc.vector.reduce_max(mx[:, 3:4], sw, AX.X))
                    nc.vector.tensor_scalar_mul(neg[:, 2:3], mx[:, 3:4], -1.0).then_inc(swm, 1)
                if i == 7:
                    dve.wait_ge(qcd, b + 1)
                    ch(nc.vector.tensor_tensor(pc[:, 0:NCS], M.PS[0:H, DB, 0:NCS],
                                               M.bias[:, 1, CLEN // 2 - 1:HALF:CSTR // 2], ALU.add))
                    ch(nc.vector.reduce_max(mx[:, 0:1], pc[:, 0:NCS], AX.X))
                    nc.vector.tensor_scalar_mul(neg[:, 0:1], mx[:, 0:1], -1.0).then_inc(cmx, 1)
                if i == 8:
                    dve.wait_ge(exc, b + 1)
                    ch(nc.vector.reciprocal(rcp[:, 0:1], sm[:, 0:1]))
                    ch(nc.vector.tensor_scalar(pc[:, 0:NCS], pc[:, 0:NCS], rcp[:, 0:1], None, ALU.mult))
                    ch(nc.vector.reduce_sum(imp[:, 0:64], pc.rearrange("h (s n) -> h s n", n=4), AX.X))
                    nc.vector.tensor_tensor(imp[:, 1:64], imp[:, 1:64], pc[:, 3:252:4], ALU.add)\
                      .then_inc(impr, 1)
                if i == 9:
                    dve.wait_ge(gsd, b + 1)
                    ch(nc.vector.tensor_copy(imp[:, 0:64], M.PS[0:H, DB, 0:64]))
                    nc.vector.memset(imp[:, 0:1], 1e9).then_inc(gsr, 1)
                    ch(nc.vector.memset(imp[:, 63:65], 1e9))
                    for n in range(TOPK // 8):
                        dve.sem_inc(pasv, 1)
                        ch(nc.vector.max(top, imp))
                        dve.sem_inc(pasv, 1)
                        ch(nc.vector.match_replace(imp, top, imp, -2e9))
                    ch(nc.vector.tensor_scalar(pen, imp, -1.5e9, MASKED, ALU.is_gt, ALU.mult))
                    dve.sem_inc(pasv, 1)
                if i == 10:
                    dve.wait_ge(qkm, b * 8 + 9)
                    dve.sem_inc(pasv, 1)
                    mask(0)
                if i == 11:
                    ch(mask(1))
                    ch(nc.vector.reduce_max(rcp[:, 1:2], mx[:, 0:3], AX.X))
                    nc.vector.tensor_scalar_mul(neg[:, 1:2], rcp[:, 1:2], -1.0).then_inc(smx, 1)
                if i == 15:
                    dve.wait_ge(exs, b + 1)
                    ch(nc.vector.tensor_tensor(sm[:, 1:2], sm[:, 1:2], sm[:, 3:4], ALU.add))
                    ch(nc.vector.reciprocal(rcp[:, 1:3], sm[:, 1:3]))
                    gates = M.sg[:, :, ds(b, 1)]
                    r3 = rcp[:, 1:3].rearrange("h (b x) -> h b x", x=1)
                    ch(nc.vector.tensor_tensor(r3, r3, gates[:, 1:3, :], ALU.mult))
                    nc.vector.tensor_copy(rcp[:, 0:1].rearrange("h (b x) -> h b x", x=1), gates[:, 0:1, :])
                    o = M.PS[0:H, DB, :]
                    dve.wait_ge(pvd, b + 2)
                    ch(nc.vector.tensor_scalar_mul(y8, o[:, P:2 * P], rcp[:, 1:2]))
                    ch(nc.vector.scalar_tensor_tensor(out=y8, in0=o[:, 2 * P:3 * P], scalar=rcp[:, 2:3], in1=y8,
                                                      op0=ALU.mult, op1=ALU.add))
                    nc.vector.scalar_tensor_tensor(out=y8, in0=o[:, 0:P], scalar=rcp[:, 0:1], in1=y8,
                                                   op0=ALU.mult, op1=ALU.add).then_inc(y8r, 1)

            def ahead(n, i):
                if i == 4:
                    queries(M.qbs, n).then_inc(qsr, 1)
                if i >= 12:
                    qk(n, i - 12)

            for i in range(NT):
                move(0, i, head=True)
                ahead(0, i)
            with dve.Fori(0, B - 1) as b:
                ch.enter(b, SAMPLE_STEPS)
                for i in range(NT):
                    move(b + 1, i)
                    if i == 0:
                        qk(b, 4)
                    tail(b, i)
                    ahead(b + 1, i)
            ch.leave(B - 1)
            qk(B - 1, 4)
            for i in range(NT):
                tail(B - 1, i)


def phase_mix_out(nc, M, A):
    ready = [M.sem(f"weights{s}_ready") for s in range(2)]
    done, moved = M.sem("tile_done"), M.sem("tile_moved")
    gla = A["w_out"][0, 0:GH * DV].rearrange("(k p) c -> p k c", p=P)
    nsa = A["w_out"][0, GH * DV:].rearrange("(q g d) c -> q d g c", q=KVH, d=HD)

    def rhs(k, c):
        return M.hT[:, k, c * CH:(c + 1) * CH]

    def load(sp, s, c):
        sp.dma_start(M.wt[:, s, 0:4, :], gla[:, :, c]).then_inc(ready[s], 16)
        for q in range(KVH):
            sp.dma_start(M.wt[q * HD:(q + 1) * HD, s, 4:8, :], nsa[q, :, :, c]).then_inc(ready[s], 16)

    with nc.Block() as block:
        @block.sync
        def _(sp):
            for s in range(2):
                load(sp, s, slice(s * P, (s + 1) * P))
            load_x(sp, M, A)
            for a, name in enumerate(("norm_mix_post", "norm_ffn_post")):
                sp.dma_start(M.rows[:, a, :], A[name].to_broadcast([P, D])).then_inc(M.sem("rows_loaded"), 16)
            with sp.Fori(1, KD // 2) as i:
                for s in range(2):
                    sp.wait_ge(done, 2 * i + (s - 1))
                    load(sp, s, ds(i * 256 + s * P, P))

        @block.tensor
        def _(pe):
            for s in range(2):
                pe.wait_ge(ready[s], 48)
                dense_tile(nc, M, pe, s, KD, rhs, done)
            with pe.Fori(1, KD // 2) as i:
                for s in range(2):
                    pe.wait_ge(ready[s], 48 * i + 48)
                    pe.wait_ge(moved, 2 * i + (s - 1))
                    dense_tile(nc, M, pe, s, KD, rhs, done)

        @block.scalar
        def _(act):
            with act.Fori(0, KD // 2) as i:
                for s in range(2):
                    act.wait_ge(done, 2 * i + (s + 1))
                    nc.scalar.activation(M.Z[:, ds(2 * i + (16 + s), 1), :].rearrange("p a (c n) -> p (a c) n", n=CH),
                                         M.PS[:, 3 * s:3 * s + 3, 0:CH], ACT.Copy).then_inc(moved, 1)


def phase_ffn(nc, M, A):
    ready = [M.sem(f"weights{s}_ready") for s in range(2)]
    done, moved = M.sem("tile_done"), M.sem("tile_moved")
    up = A["w_ff_up"][0].rearrange("(k p) c -> p k c", p=P)
    KH = DFF // 2 // P
    down = A["w_ff_down"][0].rearrange("(f k p) c -> f p k c", f=2, p=P)
    relu = M.sem("ffn_relu")

    def banks(s):
        return M.PS[:, 3 * s:3 * s + 3, 0:CH]

    def z_tile(n):
        return M.Z[:, ds(n, 1), :].rearrange("p a (c n) -> p (a c) n", n=CH)

    segments = [(0, False, KD, KH), (0, True, KD + KH, KD), (1, False, 2 * KD + KH, KH),
                (1, True, 2 * (KD + KH), KD)]
    ready0 = (48 - 16) * KD // 2

    with nc.Block() as block:
        @block.sync
        def _(sp):
            for f, is_down, g, n in segments:
                with sp.Fori(1 if g == KD else 0, n // 2) as i:
                    for s in range(2):
                        sp.wait_ge(done, 2 * i + (g + s + 1))
                        if is_down:
                            sp.dma_start(M.wt[:, s, 0:KH, :], down[f, :, :, ds(i * 256 + s * P, P)])\
                              .then_inc(ready[s], 16)
                        else:
                            sp.dma_start(M.wt[:, s, 0:KD, :], up[:, :, ds(i * 256 + (f * KH + s) * P, P)])\
                              .then_inc(ready[s], 16)

        @block.tensor
        def _(pe):
            pe.sem_inc(done, 2)
            for f, is_down, g, n in segments:
                src = M.Z if is_down else M.hT
                if is_down:
                    pe.wait_ge(moved, g + 2)
                with pe.Fori(0, n // 2) as i:
                    for s in range(2):
                        pe.wait_ge(ready[s], 16 * i + (16 * (g // 2 + 1) + ready0))
                        pe.wait_ge(moved, 2 * i + (g + s + 1))
                        dense_tile(nc, M, pe, s, KH if is_down else KD,
                                   lambda k, c: src[:, k, c * CH:(c + 1) * CH], done)

        @block.scalar
        def _(act):
            for f, is_down, g, n in segments:
                if not is_down:
                    with act.Fori(0, n // 2) as i:
                        for s in range(2):
                            act.wait_ge(done, 2 * i + (g + s + 3))
                            nc.scalar.activation(z_tile(2 * i + s), banks(s), ACT.Relu).then_inc(relu, 1)

        @block.vector
        def _(dve):
            dve.sem_inc(moved, 2)
            for f, is_down, g, n in segments:
                with dve.Fori(0, n // 2) as i:
                    for s in range(2):
                        if is_down:
                            dve.wait_ge(done, 2 * i + (g + s + 3))
                        else:
                            dve.wait_ge(relu, 2 * i + (f * KH + s + 1))
                        bank, out = banks(s), z_tile(2 * i + (16 * is_down + s))
                        if not is_down:
                            last = nc.vector.tensor_tensor(out, out, out, ALU.mult)
                        elif f == 0:
                            last = nc.vector.tensor_copy(out, bank)
                        else:
                            last = nc.vector.tensor_tensor(out, bank, out, ALU.add)
                        last.then_inc(moved, 1)


OUTS = [
    ("y_prompt", (1, T, D)),
    ("y_sample", (B, 1, D)),
    ("kv_prompt", (1, 1, T, 4, KVH, HD)),
    ("kv_sample", (1, B, 1, 4, KVH, HD)),
    ("win_prompt", (1, 1, WIN, 2, KVH, HD)),
    ("win_sample", (1, B, WIN, 2, KVH, HD)),
    ("gla_prompt", (1, 1, GH, DK, DV)),
    ("gla_sample", (1, B, GH, DK, DV)),
]


def build(nc, A, O):
    M = Mem()
    with ExitStack() as ctx:
        layout(nc, ctx, M)
        phase_load(nc, M, A, O)
        phase_norms(nc, M, A, O, 0, None, M.nw[:, 0])
        phase_project(nc, M, A)
        phase_kv_rows(nc, M, A, O)
        phase_gla(nc, M, A, O)
        phase_compress(nc, M, A)
        phase_attend(nc, M)
        phase_sample_setup(nc, M, A, O)
        phase_sample(nc, M, A, O)
        phase_mix_out(nc, M, A)
        phase_norms(nc, M, A, O, 1, M.rows[:, 0, :], M.nw[:, 1])
        phase_ffn(nc, M, A)
        phase_norms(nc, M, A, O, 2, M.rows[:, 1, :], None)


def kernel(**inputs):
    import numpy as np
    import concourse.bacc as bacc
    from concourse.bass_utils import run_bass_kernel_spmd

    nc = bacc.Bacc("TRN2", target_bir_lowering=False, num_devices=1)
    arrays, A, O = {}, {}, {}
    for name, x in inputs.items():
        x = np.ascontiguousarray(x)
        arrays[f"in_{name}"] = x
        A[name] = nc.dram_tensor(f"in_{name}", x.shape, mybir.dt.from_np(x.dtype), kind="ExternalInput").ap()
    for name, shape in OUTS:
        O[name] = nc.dram_tensor(f"out_{name}", shape, FP32, kind="ExternalOutput").ap()
    build(nc, A, O)
    r = run_bass_kernel_spmd(nc, [arrays], core_ids=[0])
    return tuple(r.results[0][f"out_{name}"] for name, _ in OUTS)
```
